# Optimizing a Trainium2 kernel written in Bass

```python
import math
import jax
import jax.numpy as jnp
from jax import lax
import numpy as np

D_MODEL = 1024
BATCH = 1
SEQ = 1024
DEPTH = 1

GRID_W = 64
CTX_LEN = 256

MLA_HEADS = 8
MLA_NOPE = 64
MLA_ROPE = 32
MLA_QK = MLA_NOPE + MLA_ROPE
MLA_V = 64
Q_LORA = 256
KV_LORA = 128

SWA_HEADS = 8
SWA_KV_HEADS = 2
SWA_GROUP = SWA_HEADS // SWA_KV_HEADS
SWA_HD = 64
WINDOW = 128
BLOCK = 128

MIX_W = MLA_HEADS * MLA_V + SWA_HEADS * SWA_HD
IN_SIZES = (Q_LORA, KV_LORA, MLA_ROPE, SWA_HEADS * SWA_HD, SWA_KV_HEADS * SWA_HD, SWA_KV_HEADS * SWA_HD)
IN_W = Q_LORA + KV_LORA + MLA_ROPE + SWA_HEADS * SWA_HD + 2 * SWA_KV_HEADS * SWA_HD
D_FF = 4 * D_MODEL
ROPE_THETA = 10000.0
EPS = 1e-6
NEG_INF = -1e30
MLA_SCALE = 1.0 / math.sqrt(MLA_QK)
SWA_SCALE = 1.0 / math.sqrt(SWA_HD)

kernel_name = "hybrid_mla_swa_dit_block"

def rmsnorm(x, g):
    xf = x.astype(jnp.float32)
    y = xf * lax.rsqrt(jnp.mean(xf * xf, axis=-1, keepdims=True) + EPS)
    return (y * g.astype(jnp.float32)).astype(x.dtype)

def modulation(cond, w_mod, b_mod):
    m = jax.nn.silu(cond) @ w_mod + b_mod
    return jnp.split(m, 6, axis=-1)

def modulate(x, g, shift, scale):
    return rmsnorm(x, g) * (1.0 + scale) + shift

def axial_rope(rows, rot_dim):
    n_freq = rot_dim // 4
    inv = ROPE_THETA ** (-jnp.arange(n_freq, dtype=jnp.float32) / n_freq)
    row = jnp.repeat(jnp.arange(rows, dtype=jnp.float32), GRID_W)
    col = jnp.tile(jnp.arange(GRID_W, dtype=jnp.float32), rows)
    ang = jnp.concatenate([row[:, None] * inv, col[:, None] * inv], axis=-1)
    return jnp.cos(ang), jnp.sin(ang)

def apply_rope(x, cos, sin):
    half = x.shape[-1] // 2
    x1, x2 = x[..., :half], x[..., half:]
    c = cos[None, :, None, :].astype(x.dtype)
    s = sin[None, :, None, :].astype(x.dtype)
    return jnp.concatenate([x1 * c - x2 * s, x2 * c + x1 * s], axis=-1)

def project(h, w_in, g_q_a, w_uq, g_kv_a, w_ukv, g_mla_q, g_mla_k, g_swa_q, g_swa_k, rope):
    B, n, _ = h.shape
    z = h @ w_in
    offs = []
    acc = 0
    for sz in IN_SIZES[:-1]:
        acc += sz
        offs.append(acc)
    cq, ckv, kr, qs, ks, vs = jnp.split(z, offs, axis=-1)
    q_m = (rmsnorm(cq, g_q_a) @ w_uq).reshape(B, n, MLA_HEADS, MLA_QK)
    q_m = rmsnorm(q_m, g_mla_q)
    kv = (rmsnorm(ckv, g_kv_a) @ w_ukv).reshape(B, n, MLA_HEADS, MLA_NOPE + MLA_V)
    k_nope, v_m = kv[..., :MLA_NOPE], kv[..., MLA_NOPE:]
    k_rope = jnp.broadcast_to(kr[:, :, None, :], (B, n, MLA_HEADS, MLA_ROPE))
    k_m = rmsnorm(jnp.concatenate([k_nope, k_rope], axis=-1), g_mla_k)
    q_s = rmsnorm(qs.reshape(B, n, SWA_HEADS, SWA_HD), g_swa_q)
    k_s = rmsnorm(ks.reshape(B, n, SWA_KV_HEADS, SWA_HD), g_swa_k)
    v_s = vs.reshape(B, n, SWA_KV_HEADS, SWA_HD)
    if rope is not None:
        (cos_m, sin_m), (cos_s, sin_s) = rope
        q_m = jnp.concatenate([q_m[..., :MLA_NOPE], apply_rope(q_m[..., MLA_NOPE:], cos_m, sin_m)], axis=-1)
        k_m = jnp.concatenate([k_m[..., :MLA_NOPE], apply_rope(k_m[..., MLA_NOPE:], cos_m, sin_m)], axis=-1)
        q_s = apply_rope(q_s, cos_s, sin_s)
        k_s = apply_rope(k_s, cos_s, sin_s)
    return q_m, k_m, v_m, q_s, k_s, v_s

def mla_latent(q, k_lat, v_lat, k_ctx, v_ctx):
    B, S = q.shape[0], q.shape[1]
    nb = S // BLOCK
    k_all = jnp.concatenate([k_ctx, k_lat], axis=1)
    v_all = jnp.concatenate([v_ctx, v_lat], axis=1)
    qb = q.reshape(B, nb, BLOCK, MLA_HEADS, MLA_QK).transpose(1, 0, 2, 3, 4)

    def one_block(qblk):
        s = jnp.einsum('bqhd,bkhd->bhqk', qblk, k_all, preferred_element_type=jnp.float32) * MLA_SCALE
        p = jax.nn.softmax(s, axis=-1).astype(v_all.dtype)
        return jnp.einsum('bhqk,bkhd->bqhd', p, v_all)

    out = lax.map(one_block, qb)
    return out.transpose(1, 0, 2, 3, 4).reshape(B, S, MLA_HEADS * MLA_V)

def mla_context(q, k, v):
    B, n = q.shape[0], q.shape[1]
    s = jnp.einsum('bqhd,bkhd->bhqk', q, k, preferred_element_type=jnp.float32) * MLA_SCALE
    p = jax.nn.softmax(s, axis=-1).astype(v.dtype)
    return jnp.einsum('bhqk,bkhd->bqhd', p, v).reshape(B, n, MLA_HEADS * MLA_V)

def swa_latent(q, k, v, k_ctx, v_ctx, sink):
    B, S = q.shape[0], q.shape[1]
    nb = S // BLOCK
    n_ctx = k_ctx.shape[1]
    qb = q.reshape(B, nb, BLOCK, SWA_KV_HEADS, SWA_GROUP, SWA_HD)
    pad = ((0, 0), (BLOCK, BLOCK), (0, 0), (0, 0))
    kp = jnp.pad(k, pad).reshape(B, nb + 2, BLOCK, SWA_KV_HEADS, SWA_HD)
    vp = jnp.pad(v, pad).reshape(B, nb + 2, BLOCK, SWA_KV_HEADS, SWA_HD)
    kband = jnp.concatenate([kp[:, :-2], kp[:, 1:-1], kp[:, 2:]], axis=2)
    vband = jnp.concatenate([vp[:, :-2], vp[:, 1:-1], vp[:, 2:]], axis=2)
    blk = jnp.arange(nb)[:, None] * BLOCK
    qpos = blk + jnp.arange(BLOCK)[None, :]
    kpos = blk - BLOCK + jnp.arange(3 * BLOCK)[None, :]
    valid = ((jnp.abs(qpos[:, :, None] - kpos[:, None, :]) <= WINDOW)
             & (kpos[:, None, :] >= 0) & (kpos[:, None, :] < S))
    s_band = jnp.einsum('bnqhgd,bnkhd->bnhgqk', qb, kband, preferred_element_type=jnp.float32) * SWA_SCALE
    s_band = jnp.where(valid[None, :, None, None], s_band, NEG_INF)
    s_ctx = jnp.einsum('bnqhgd,bkhd->bnhgqk', qb, k_ctx, preferred_element_type=jnp.float32) * SWA_SCALE
    s_sink = jnp.broadcast_to(
        sink.astype(jnp.float32).reshape(SWA_KV_HEADS, SWA_GROUP)[None, None, :, :, None, None],
        s_band.shape[:-1] + (1,))
    p = jax.nn.softmax(jnp.concatenate([s_band, s_ctx, s_sink], axis=-1), axis=-1)
    p_band = p[..., :3 * BLOCK].astype(v.dtype)
    p_ctx = p[..., 3 * BLOCK:3 * BLOCK + n_ctx].astype(v.dtype)
    out = (jnp.einsum('bnhgqk,bnkhd->bnqhgd', p_band, vband)
           + jnp.einsum('bnhgqk,bkhd->bnqhgd', p_ctx, v_ctx))
    return out.reshape(B, S, SWA_HEADS * SWA_HD)

def swa_context(q, k, v, sink):
    B, n = q.shape[0], q.shape[1]
    qg = q.reshape(B, n, SWA_KV_HEADS, SWA_GROUP, SWA_HD)
    s = jnp.einsum('bqhgd,bkhd->bhgqk', qg, k, preferred_element_type=jnp.float32) * SWA_SCALE
    s_sink = jnp.broadcast_to(
        sink.astype(jnp.float32).reshape(SWA_KV_HEADS, SWA_GROUP)[None, :, :, None, None],
        s.shape[:-1] + (1,))
    p = jax.nn.softmax(jnp.concatenate([s, s_sink], axis=-1), axis=-1)[..., :n].astype(v.dtype)
    return jnp.einsum('bhgqk,bkhd->bqhgd', p, v).reshape(B, n, SWA_HEADS * SWA_HD)

def squared_relu_mlp(h, w1, w2):
    a = jax.nn.relu(h @ w1)
    return (a * a) @ w2

def setup_inputs(seed: int = 0) -> dict:
    key = jax.random.key(seed)
    ks = jax.random.split(key, 24)
    f32 = jnp.float32

    def w(k, shape, fan_in):
        return jax.random.normal(k, shape, f32) * (fan_in ** -0.5)

    def gain(k, shape):
        return 1.0 + 0.1 * jax.random.normal(k, shape, f32)

    L = DEPTH
    return {
        "x": jax.random.normal(ks[0], (BATCH, SEQ, D_MODEL), f32),
        "c": jax.random.normal(ks[1], (BATCH, D_MODEL), f32),
        "ctx": jax.random.normal(ks[2], (BATCH, CTX_LEN, D_MODEL), f32),
        "c_ctx": jax.random.normal(ks[3], (D_MODEL,), f32),
        "w_mod": w(ks[4], (L, D_MODEL, 6 * D_MODEL), D_MODEL),
        "b_mod": 0.01 * jax.random.normal(ks[5], (L, 6 * D_MODEL), f32),
        "g_attn": gain(ks[6], (L, D_MODEL)),
        "w_in": w(ks[7], (L, D_MODEL, IN_W), D_MODEL),
        "g_q_a": gain(ks[8], (L, Q_LORA)),
        "w_uq": w(ks[9], (L, Q_LORA, MLA_HEADS * MLA_QK), Q_LORA),
        "g_kv_a": gain(ks[10], (L, KV_LORA)),
        "w_ukv": w(ks[11], (L, KV_LORA, MLA_HEADS * (MLA_NOPE + MLA_V)), KV_LORA),
        "g_mla_q": gain(ks[12], (L, MLA_QK)),
        "g_mla_k": gain(ks[13], (L, MLA_QK)),
        "g_swa_q": gain(ks[14], (L, SWA_HD)),
        "g_swa_k": gain(ks[15], (L, SWA_HD)),
        "swa_sink": 0.5 * jax.random.normal(ks[16], (L, SWA_HEADS), f32),
        "w_out": w(ks[17], (L, MIX_W, D_MODEL), MIX_W),
        "g_mlp": gain(ks[18], (L, D_MODEL)),
        "w_mlp1": w(ks[19], (L, D_MODEL, D_FF), D_MODEL),
        "w_mlp2": w(ks[20], (L, D_FF, D_MODEL), D_FF),
    }

def reference(x, c, ctx, c_ctx, w_mod, b_mod, g_attn, w_in, g_q_a, w_uq, g_kv_a, w_ukv,
              g_mla_q, g_mla_k, g_swa_q, g_swa_k, swa_sink, w_out, g_mlp, w_mlp1, w_mlp2):
    rows = x.shape[1] // GRID_W
    rope = (axial_rope(rows, MLA_ROPE), axial_rope(rows, SWA_HD))

    for i in range(DEPTH):
        sh1, sc1, g1, sh2, sc2, g2 = [m[:, None, :] for m in modulation(c, w_mod[i], b_mod[i])]
        csh1, csc1, cg1, csh2, csc2, cg2 = modulation(c_ctx, w_mod[i], b_mod[i])

        h_lat = modulate(x, g_attn[i], sh1, sc1)
        h_ctx = modulate(ctx, g_attn[i], csh1, csc1)
        proj_args = (w_in[i], g_q_a[i], w_uq[i], g_kv_a[i], w_ukv[i],
                     g_mla_q[i], g_mla_k[i], g_swa_q[i], g_swa_k[i])
        qm_l, km_l, vm_l, qs_l, ks_l, vs_l = project(h_lat, *proj_args, rope)
        qm_c, km_c, vm_c, qs_c, ks_c, vs_c = project(h_ctx, *proj_args, None)

        mix_lat = jnp.concatenate([
            mla_latent(qm_l, km_l, vm_l, km_c, vm_c),
            swa_latent(qs_l, ks_l, vs_l, ks_c, vs_c, swa_sink[i]),
        ], axis=-1)
        x = x + g1 * (mix_lat @ w_out[i])
        x = x + g2 * squared_relu_mlp(modulate(x, g_mlp[i], sh2, sc2), w_mlp1[i], w_mlp2[i])

        if i + 1 < DEPTH:
            mix_ctx = jnp.concatenate([
                mla_context(qm_c, km_c, vm_c),
                swa_context(qs_c, ks_c, vs_c, swa_sink[i]),
            ], axis=-1)
            ctx = ctx + cg1 * (mix_ctx @ w_out[i])
            ctx = ctx + cg2 * squared_relu_mlp(modulate(ctx, g_mlp[i], csh2, csc2), w_mlp1[i], w_mlp2[i])

    return x


_drawn_inputs = setup_inputs


def setup_inputs(seed=0):
    import zlib

    import numpy as np

    out = dict(_drawn_inputs(seed))
    spreads = {}
    factors = {'b_mod': 3.18,
     'g_attn': 5.921,
     'g_q_a': 8.0,
     'g_mla_q': 8.0,
     'g_mla_k': 8.0,
     'g_swa_q': 8.0,
     'g_swa_k': 8.0,
     'swa_sink': 8.0}
    for name, (base, spread) in spreads.items():
        noise = np.random.default_rng([zlib.crc32(name.encode()), seed]).standard_normal(out[name].shape)
        drawn = base * np.exp(spread * noise) if base else spread * noise
        out[name] = jnp.asarray(drawn.astype(out[name].dtype))
    for name, factor in factors.items():
        out[name] = (out[name] * factor).astype(out[name].dtype)
    return out
```

```python
from contextlib import ExitStack

import concourse.bass as bass
from concourse import mybir

F32 = mybir.dt.float32
F32R = mybir.dt.float32r
ALU = mybir.AluOpType
ACT = mybir.ActivationFunctionType
AX = mybir.AxisListType

P = 128
BANK = 512
D = 1024
KC = D // P
SEQ = 1024
CTX = 256
NT = (SEQ + CTX) // P
NCT = CTX // P
NB = SEQ // P
HEADS = 8
NOPE, ROPE, QK, VD = 64, 32, 96, 64
QL, KVL = 256, 128
SH, SKV, SD = 8, 2, 64
IN_W = QL + KVL + ROPE + SH * SD + 2 * SKV * SD
FF = 4096
NF = FF // P
KALL = SEQ + CTX
EPS = 1e-6
MLA_SCALE = QK ** -0.5
SWA_SCALE = SD ** -0.5
NS = SH + SKV
ZCH = ((0, 416), (416, 928), (928, 1184))
SPILLS = 9
UNITK = 5
GRP = SH // SKV


class Chain:

    def __init__(self, eng, sem):
        self.eng, self.sem, self.n, self.base = eng, sem, 0, 0

    def __call__(self, ins):
        self.n += 1
        ins.then_inc(self.sem, 1)
        self.eng.wait_ge(self.sem, self.base + self.n)

    def enter(self, turn, per):
        self.start, self.per = self.base + self.n, per
        self.base, self.n = self.start + turn * per, 0

    def leave(self, turns):
        assert self.n == self.per, ("instructions per turn", self.n)
        self.base, self.n = self.start + turns * self.per, 0


def bc(ap, n):
    return ap.unsqueeze(len(ap.shape)).to_broadcast(tuple(ap.shape) + (n,))


def mid(ap, n):
    return ap.unsqueeze(1).to_broadcast((ap.shape[0], n, ap.shape[1]))


def flat(ap):
    return ap.rearrange("p a b -> p (a b)")


def modulation_phase(nc, A, scr):
    NW = 6 * D
    WR = 4
    with ExitStack() as ctx:
        sb = lambda n, s, d=F32: ctx.enter_context(nc.sbuf_tensor(n, s, d))
        sem = lambda n: ctx.enter_context(nc.semaphore(n))
        wm = sb("m_w", [P, WR, NW])
        cc = sb("m_c", [P, KC, 2])
        ex = sb("m_e", [P, KC, 2])
        sT = sb("m_s", [P, KC, 32])
        bm = sb("m_b", [P, 3, BANK])
        mo = sb("m_o", [P, 3, BANK])
        ps = ctx.enter_context(nc.psum_tensor("m_ps", [P, 3, BANK], F32))
        c_loaded = sem("m_c_loaded")
        b_loaded = sem("m_b_loaded")
        w_loaded = [sem(f"m_w_loaded{i}") for i in range(WR)]
        cleared = sem("m_cleared")
        exped = sem("m_exped")
        silu_ready = sem("m_silu_ready")
        chain = sem("m_chain")
        w_used = sem("m_w_used")
        summed = sem("m_summed")
        stored = sem("m_stored")
        block = ctx.enter_context(nc.Block())

        @block.sync
        def _(sp):
            with nc.allow_non_contiguous_dma(reason="two small vectors"):
                sp.dma_start(cc[:, :, 0], A["c"].rearrange("b (k p) -> p (b k)", p=P)).then_inc(c_loaded, 16)
                sp.dma_start(cc[:, :, 1], A["c_ctx"].rearrange("(k p) -> p k", p=P)).then_inc(c_loaded, 16)
            for k in range(KC):
                if k >= WR:
                    sp.wait_ge(w_used, k - WR + 1)
                sp.dma_start(wm[:, k % WR, :], A["w_mod"][0, k * P:(k + 1) * P, :]).then_inc(w_loaded[k % WR], 16)
            sp.wait_ge(summed, 1)
            for j in range(4):
                sp.dma_start(scr["mod"].rearrange("r (b j n) -> j r b n", b=3, j=4)[j],
                             mo[32 * j:32 * j + 2, :, :]).then_inc(stored, 16)
            sp.wait_ge(stored, 64)

        @block.gpsimd
        def _(pool):
            nc.gpsimd.memset(flat(sT[:, :, :]), 0.0).then_inc(cleared, 1)
            nc.gpsimd.memset(flat(bm[:, :, :]), 0.0).then_inc(cleared, 1)
            pool.wait_ge(cleared, 2)
            for j in range(4):
                for r in range(2):
                    pool.dma_start(bm[32 * j + r:32 * j + r + 1, :, :],
                                   A["b_mod"].rearrange("l (b j n) -> j l b n", b=3, j=4)[j]).then_inc(b_loaded, 16)

        @block.scalar
        def _(act):
            act.wait_ge(c_loaded, 32)
            nc.scalar.activation(flat(ex[:, :, :]), flat(cc[:, :, :]), ACT.Exp, scale=-1.0).then_inc(exped, 1)

        @block.vector
        def _(dve):
            link = Chain(dve, chain)
            dve.wait_ge(exped, 1)
            link(nc.vector.tensor_scalar_add(flat(ex[:, :, :]), flat(ex[:, :, :]), 1.0))
            link(nc.vector.reciprocal(flat(ex[:, :, :]), flat(ex[:, :, :])))
            dve.wait_ge(cleared, 1)
            nc.vector.tensor_tensor(sT[:, :, 0:2], cc[:, :, :], ex[:, :, :], ALU.mult).then_inc(silu_ready, 1)
            dve.wait_ge(w_used, KC)
            dve.wait_ge(b_loaded, 128)
            nc.vector.tensor_tensor(flat(mo[:, :, :]), flat(ps[:, :, :]), flat(bm[:, :, :]), ALU.add).then_inc(summed, 1)

        @block.tensor
        def _(pe):
            pe.wait_ge(silu_ready, 1)
            for k in range(KC):
                pe.wait_ge(w_loaded[k % WR], 16 * (k // WR + 1))
                for n in range(12):
                    j = n % 4
                    last = nc.tensor.matmul(ps[32 * j:32 * j + 32, n // 4, :], sT[:, k, :],
                                            wm[:, k % WR, n * BANK:(n + 1) * BANK], start=(k == 0), stop=(k == KC - 1))
                last.then_inc(w_used, 1)


def token_phase(nc, A, scr):
    with ExitStack() as ctx:
        sb = lambda n, s, d=F32: ctx.enter_context(nc.sbuf_tensor(n, s, d))
        sem = lambda n: ctx.enter_context(nc.semaphore(n))
        w_in = [sb(f"w_in{i}", [P, KC, IN_W], F32R) for i in range(2)]
        w_uq = [sb(f"w_uq{i}", [P, 2, HEADS * QK], F32R) for i in range(2)]
        w_kv = [sb(f"w_kv{i}", [P, HEADS * P], F32R) for i in range(2)]

        with ExitStack() as prep:
            WR = 4
            raw = prep.enter_context(nc.sbuf_tensor("w_raw", [P, WR, IN_W], F32))
            loaded = [prep.enter_context(nc.semaphore(f"wp_loaded{i}")) for i in range(WR)]
            hi_done = prep.enter_context(nc.semaphore("wp_hi_done"))
            lo_done = prep.enter_context(nc.semaphore("wp_lo_done"))
            jobs = [(A["w_in"][0, k * P:(k + 1) * P, :], w_in[0][:, k, :], w_in[1][:, k, :], IN_W) for k in range(KC)]
            jobs += [(A["w_uq"][0, k * P:(k + 1) * P, :], w_uq[0][:, k, :], w_uq[1][:, k, :], HEADS * QK) for k in range(2)]
            jobs += [(A["w_ukv"][0], w_kv[0][:, :], w_kv[1][:, :], HEADS * P)]
            block = prep.enter_context(nc.Block())

            @block.sync
            def _(sp):
                for i, (src, _, _, n) in enumerate(jobs):
                    if i >= WR:
                        sp.wait_ge(lo_done, i - WR + 1)
                    sp.dma_start(raw[:, i % WR, 0:n], src).then_inc(loaded[i % WR], 16)

            @block.scalar
            def _(act):
                for i, (_, hi, _, n) in enumerate(jobs):
                    act.wait_ge(loaded[i % WR], 16 * (i // WR + 1))
                    nc.scalar.activation(hi, raw[:, i % WR, 0:n], ACT.Copy).then_inc(hi_done, 1)

            @block.vector
            def _(dve):
                for i, (_, hi, lo, n) in enumerate(jobs):
                    dve.wait_ge(hi_done, i + 1)
                    nc.vector.tensor_tensor(lo, raw[:, i % WR, 0:n], hi.bitcast(F32), ALU.subtract).then_inc(lo_done, 1)

        ident = sb("t_ident", [P, P])
        xt = sb("t_x", [P, 2, D])
        tab = sb("t_rope", [P, 2, 2 * (ROPE + SD)])
        xn = sb("t_xn", [P, KC, P])
        junk = sb("t_junk", [P, D])
        hT = [sb(f"t_h{i}", [P, KC, P], F32R) for i in range(2)]
        zs = sb("t_z", [P, IN_W])
        qm = sb("t_q", [P, HEADS, QK])
        kv = sb("t_kv", [P, HEADS, P])
        sqq = sb("t_sqq", [P, HEADS, QK])
        sqk = sb("t_sqk", [P, HEADS, NOPE])
        sqs = sb("t_sqs", [P, NS, SD])
        gq = sb("t_gq", [P, HEADS, QK])
        gk = sb("t_gk", [P, HEADS, NOPE])
        gs = sb("t_gs", [P, NS, SD])
        gr = sb("t_gr", [P, 1, ROPE])
        swq = sb("t_swq", [P, HEADS, ROPE])
        sws = sb("t_sws", [P, NS, SD])
        swr = sb("t_swr", [P, 1, ROPE])
        roq = sb("t_roq", [P, HEADS, ROPE])
        ros = sb("t_ros", [P, NS, SD])
        ror = sb("t_ror", [P, 1, ROPE])
        qn = sb("t_qn", [P, HEADS, QK])
        kn = sb("t_kn", [P, HEADS, QK])
        sn = sb("t_sn", [P, SH + 2 * SKV, SD])
        cn = sb("t_cn", [P, 3, P])
        cT = [sb(f"t_c{i}", [P, 3, P], F32R) for i in range(2)]
        qT = sb("t_qT", [QK, 2, HEADS, P], F32R)
        kT = sb("t_kT", [QK, 2, HEADS, P], F32R)
        sT = sb("t_sT", [P, SH, P], F32R)
        sK = sb("t_sK", [P, 2, SKV, P], F32R)
        vm = sb("t_vm", [P, HEADS, 2 * VD], F32R)
        vs = sb("t_vs", [P, SKV, 2 * SD], F32R)
        stx = sb("t_stx", [P, 1])
        stc = sb("t_stc", [P, 2])
        stn = sb("t_stn", [P, 27])
        mcol = sb("t_mcol", [P, 2, 2, KC])
        gcol = sb("t_gcol", [P, KC])
        b_qa = sb("t_bqa", [P, QL])
        b_kva = sb("t_bkva", [P, KVL])
        b_mq = sb("t_bmq", [P, QK])
        b_mk = sb("t_bmk", [P, QK])
        b_sq = sb("t_bsq", [P, SD])
        b_sk = sb("t_bsk", [P, SD])
        zero = sb("t_zero", [P, 2, SKV, P])
        ps = ctx.enter_context(nc.psum_tensor("t_ps", [P, 8, BANK], F32))
        TB, UB = 3, 5

        consts = sem("t_consts")
        mod_ready = sem("t_mod_ready")
        zeroed = sem("t_zeroed")
        x_loaded = [sem(f"t_x_loaded{i}") for i in range(2)]
        tab_loaded = [sem(f"t_tab_loaded{i}") for i in range(2)]
        squared = sem("t_squared")
        var_ready = sem("t_var_ready")
        root_ready = sem("t_root_ready")
        xn_ready = sem("t_xn_ready")
        filled = sem("t_filled")
        emptied = sem("t_emptied")
        hi_ready = sem("t_hi_ready")
        hv_ready = sem("t_hv_ready")
        h_hi = sem("t_h_hi")
        h_ready = sem("t_h_ready")
        z_ready = sem("t_z_ready")
        z_copied = sem("t_z_copied")
        c_ready = sem("t_c_ready")
        u_ready = sem("t_u_ready")
        u_copied = sem("t_u_copied")
        gained = sem("t_gained")
        normed = sem("t_normed")
        v_hi = sem("t_v_hi")
        spilled = sem("t_spilled")
        pads = sem("t_pads")
        v_chain = sem("t_v_chain")
        g_chain = sem("t_g_chain")
        def FILL(t, k):
            if isinstance(t, int) and t >= NT - 1 and k > 6:
                return 10 * t - 5 + 7
            if isinstance(t, int) and t == NT:
                return 10 * t - 5 + k - 2
            return t * 10 + (k - 5)

        def HI(t, k):
            return t * 8 + (k - 7 if k < 7 else 0)

        def EV(t, k):
            last = isinstance(t, int) and t == NT - 1
            return t * 3 + k + 1 - (1 if last and k > 0 else 0)

        block = ctx.enter_context(nc.Block())

        @block.sync
        def _(sp):
            def load_x(t, b):
                src = A["ctx"][0, t * P:(t + 1) * P, :] if isinstance(t, int) and t < NCT else \
                    A["x"][0, bass.ds((t - NCT) * P, P), :]
                sp.dma_start(xt[:, b, :], src).then_inc(x_loaded[b], 16)

            def load_tab(t, b):
                sp.dma_start(tab[:, b, :], A["rope"][bass.ds(t * P, P), :]).then_inc(tab_loaded[b], 16)

            def step(t, b, load=True):
                if load and not (isinstance(t, int) and t > NT - 3):
                    sp.wait_ge(xn_ready, t + 1)
                    load_x(t + 2, b)
                if load:
                    if not (isinstance(t, int) and t == 0):
                        sp.wait_ge(normed, t)
                    load_tab(t + 1, 1 - b)
                if isinstance(t, int) and t == 0:
                    return
                u = t - 1
                sp.wait_ge(emptied, FILL(t, 6) + 1)
                cols = bass.ds(u * P, P)
                for i in range(2):
                    sp.dma_start(scr["q"][:, :, i, cols].rearrange("h p c -> p h c"),
                                 qT[:, i, :, :].bitcast(F32)).then_inc(spilled, 16)
                    sp.dma_start(scr["k"][:, :, i, cols].rearrange("h p c -> p h c"),
                                 kT[:, i, :, :].bitcast(F32)).then_inc(spilled, 16)
                    kcols = bass.ds(u * P + (0 if isinstance(u, int) and u < NCT else P), P)
                    sp.dma_start(scr["sk"][:, i, :, kcols].rearrange("v p c -> p v c"),
                                 sK[:, i, :, :].bitcast(F32)).then_inc(spilled, 16)
                sp.dma_start(scr["sq"][bass.ds(u, 1)].rearrange("a p c -> p (a c)"),
                             sT[:, :, :].rearrange("p h c -> p (h c)").bitcast(F32)).then_inc(spilled, 16)
                sp.dma_start(scr["v"][:, bass.ds(u, 1), :, :].rearrange("h a p c -> p (h a) c"),
                             vm[:, :, :].bitcast(F32)).then_inc(spilled, 16)
                vt = u if isinstance(u, int) and u < NCT else u + 1
                sp.dma_start(scr["sv"][bass.ds(vt, 1)].rearrange("a p c -> p (a c)"),
                             flat(vs[:, :, :]).bitcast(F32)).then_inc(spilled, 16)

            load_x(0, 0)
            load_tab(0, 0)
            load_x(1, 1)
            sp.dma_start(ident[:, :], A["ident"]).then_inc(consts, 16)
            for dst, name in ((b_qa, "g_q_a"), (b_kva, "g_kv_a"), (b_mq, "g_mla_q"), (b_mk, "g_mla_k"),
                              (b_sq, "g_swa_q"), (b_sk, "g_swa_k")):
                sp.dma_start(dst[:, :], A[name].partition_broadcast(P).rearrange("p a n -> p (a n)")).then_inc(consts, 16)
            with nc.allow_non_contiguous_dma(reason="a few vectors, one element a row"):
                sp.dma_start(gcol[:, :], A["g_attn"].rearrange("l (k p) -> p (l k)", p=P)).then_inc(consts, 16)
                for s in range(2):
                    for r in range(2):
                        sp.dma_start(mcol[:, s, r, :],
                                     scr["mod"][r, s * D:(s + 1) * D].rearrange("(k p) -> p k", p=P)).then_inc(consts, 16)
            for t in range(NT + 1):
                step(t, t % 2, load=t < NT - 1)
            sp.wait_ge(zeroed, 1)
            for e in (CTX, CTX + P + SEQ):
                sp.dma_start(scr["sk"][:, :, :, e:e + P].rearrange("v i p c -> p (v i) c"),
                             zero[:, :, :, :].rearrange("p i v c -> p (i v) c")).then_inc(pads, 16)
            for e in (NCT, NT + 1):
                sp.dma_start(scr["sv"][e], zero[:, :, :, :].rearrange("p i v c -> p (i v c)")[:, 0:SKV * P]).then_inc(pads, 16)
            sp.wait_ge(pads, 64)
            sp.wait_ge(spilled, 16 * SPILLS * NT)

        @block.gpsimd
        def _(pool):
            link = Chain(pool, g_chain)
            nc.gpsimd.memset(zero[:, :, :, :].rearrange("p i v c -> p (i v c)"), 0.0).then_inc(zeroed, 1)
            pool.wait_ge(consts, 16 * 12)

            def swap(out, x, sin, n, h):
                nc.gpsimd.tensor_tensor(out[:, :, 0:h], x[:, :, h:2 * h], mid(sin[:, 0:h], n), ALU.mult)
                return nc.gpsimd.tensor_tensor(out[:, :, h:2 * h], x[:, :, 0:h], mid(sin[:, h:2 * h], n), ALU.mult)

            def step(t, b, turn):
                pool.wait_ge(z_copied, t * 3 + 3)
                if not (isinstance(t, int) and t == 0):
                    pool.wait_ge(normed, t)
                nc.gpsimd.tensor_tensor(gs[:, 0:SH, :], zs[:, 416:928].rearrange("p (h d) -> p h d", h=SH),
                                        mid(b_sq[:, :], SH), ALU.mult)
                nc.gpsimd.tensor_tensor(gs[:, SH:NS, :], zs[:, 928:1056].rearrange("p (h d) -> p h d", h=SKV),
                                        mid(b_sk[:, :], SKV), ALU.mult)
                link(nc.gpsimd.tensor_tensor(gr[:, 0, :], zs[:, 384:416], b_mk[:, NOPE:QK], ALU.mult))
                pool.wait_ge(tab_loaded[b], turn * 16 + 16)
                tb = tab[:, b, :]
                swap(swr, gr, tb[:, ROPE:2 * ROPE], 1, ROPE // 2)
                swap(sws, gs, tb[:, 2 * ROPE + SD:], NS, SD // 2)
                pool.wait_ge(u_copied, t * 4 + 4)
                link(nc.gpsimd.tensor_tensor(gq[:, :, :], qm[:, :, :], mid(b_mq[:, :], HEADS), ALU.mult))
                nc.gpsimd.tensor_tensor(gk[:, :, :], kv[:, :, 0:NOPE], mid(b_mk[:, 0:NOPE], HEADS), ALU.mult)
                swap(swq, gq[:, :, NOPE:QK], tb[:, ROPE:2 * ROPE], HEADS, ROPE // 2).then_inc(gained, 1)

            for t in range(2):
                step(t, t, 0)
            with pool.Fori(1, NT // 2) as i:
                link.enter(i - 1, 4)
                step(i * 2, 0, i)
                step(i * 2 + 1, 1, i)
                link.leave(NT // 2 - 1)

        @block.scalar
        def _(act):
            def root(e, st):
                act.wait_ge(var_ready, e + 1)
                nc.scalar.activation(st, st, ACT.Sqrt).then_inc(root_ready, 1)

            def stat_x(e, b, turn):
                act.wait_ge(x_loaded[b], turn * 16 + 16)
                nc.scalar.activation(junk[:, :], xt[:, b, :], ACT.Square, accum_out=stx[:, :]).then_inc(squared, 1)
                root(e, stx[:, :])

            def hi_fills(t):
                for k in range(7):
                    n = FILL(t, k)
                    src = ps[:, TB + (k + 1) % 2, :]
                    act.wait_ge(filled, n + 1)
                    if k == 0 and not (isinstance(t, int) and t == 1):
                        act.wait_ge(spilled, (t - 1) * 16 * SPILLS)
                    if k < 4:
                        o = (qT, kT)[k // 2][:, 0, 4 * (k % 2):4 * (k % 2) + 4, :]
                        ins = nc.scalar.activation(o.rearrange("p h c -> p (h c)"), src[0:QK, :], ACT.Copy)
                    elif k < 6:
                        for r in range(2):
                            ins = nc.scalar.activation(sT[0:SD, 4 * (k - 4):4 * (k - 4) + 4, :].rearrange("p (g r) c -> p r g c", r=2)[:, r],
                                                       src[SD * r:SD * r + SD, 0:2 * P].rearrange("p (g c) -> p g c", g=2), ACT.Copy)
                    else:
                        ins = nc.scalar.activation(flat(sK[:, 0, :, :]), src[:, 0:SKV * P], ACT.Copy)
                    ins.then_inc(hi_ready, 1)

            def step(t, b, turn, nturn):
                first = isinstance(t, int) and t == 0
                last = isinstance(t, int) and t == NT - 1
                if not last:
                    stat_x(EV(t, 0), 1 - b, nturn)
                if not first:
                    act.wait_ge(normed, t)
                for j, (lo, hi) in enumerate(ZCH):
                    act.wait_ge(z_ready, t * 3 + j + 1)
                    nc.scalar.activation(zs[:, lo:hi], ps[:, j, 0:hi - lo], ACT.Copy).then_inc(z_copied, 1)
                act.wait_ge(z_copied, t * 3 + 3)
                nc.scalar.activation(sqs[:, :, :].rearrange("p h d -> p (h d)"), zs[:, 416:1056], ACT.Square)
                nc.scalar.activation(junk[:, 384:416], zs[:, 384:416], ACT.Square, accum_out=stn[:, 26:27])
                nc.scalar.activation(junk[:, 0:QL], zs[:, 0:QL], ACT.Square, accum_out=stc[:, 0:1])
                nc.scalar.activation(junk[:, QL:384], zs[:, QL:384], ACT.Square, accum_out=stc[:, 1:2]).then_inc(squared, 1)
                root(EV(t, 1), stc[:, :])
                if not first:
                    hi_fills(t)
                if not last:
                    act.wait_ge(hv_ready, t + 2)
                    nc.scalar.activation(flat(hT[0][:, :, :]), flat(xn[:, :, :]), ACT.Copy).then_inc(h_hi, 1)
                act.wait_ge(filled, FILL(t, 9) + 1)
                nc.scalar.activation(flat(cT[0][:, :, :]), ps[:, TB, 0:3 * P], ACT.Copy).then_inc(hi_ready, 1)
                for j in range(4):
                    act.wait_ge(u_ready, t * 4 + j + 1)
                    if j < 2:
                        nc.scalar.activation(flat(qm[:, 4 * j:4 * j + 4, :]), ps[:, UB + j, 0:4 * QK],
                                             ACT.Copy).then_inc(u_copied, 1)
                    else:
                        nc.scalar.activation(flat(kv[:, 4 * j - 8:4 * j - 4, :]), ps[:, UB + j % 3 if j < 3 else UB, :],
                                             ACT.Copy).then_inc(u_copied, 1)
                act.wait_ge(u_copied, t * 4 + 4)
                nc.scalar.activation(flat(sqq[:, :, :]), flat(qm[:, :, :]), ACT.Square)
                nc.scalar.activation(sqk[:, :, :], kv[:, :, 0:NOPE], ACT.Square).then_inc(squared, 1)
                if not first:
                    act.wait_ge(spilled, t * 16 * SPILLS)
                nc.scalar.activation(vm[:, :, 0:VD], kv[:, :, NOPE:P], ACT.Copy)
                nc.scalar.activation(vs[:, :, 0:SD], zs[:, 1056:1184].rearrange("p (v d) -> p v d", v=SKV),
                                     ACT.Copy).then_inc(v_hi, 1)
                root(EV(t, 2), stn[:, 0:26])

            stat_x(0, 0, 0)
            act.wait_ge(hv_ready, 1)
            nc.scalar.activation(flat(hT[0][:, :, :]), flat(xn[:, :, :]), ACT.Copy).then_inc(h_hi, 1)
            step(0, 0, 0, 0)
            step(1, 1, 0, 1)
            with act.Fori(1, NT // 2 - 1) as i:
                step(i * 2, 0, i, i)
                step(i * 2 + 1, 1, i, i + 1)
            step(NT - 2, 0, NT // 2 - 1, NT // 2 - 1)
            step(NT - 1, 1, NT // 2 - 1, None)
            hi_fills(NT)

        @block.vector
        def _(dve):
            V = nc.vector
            link = Chain(dve, v_chain)

            def x_norm(e, t, b):
                dve.wait_ge(squared, e + 1)
                V.tensor_scalar(stx[:, :], stx[:, :], 1.0 / D, EPS, ALU.mult, ALU.add).then_inc(var_ready, 1)
                dve.wait_ge(root_ready, e + 1)
                link(V.reciprocal(stx[:, :], stx[:, :]))
                if not (isinstance(t, int) and t == 0):
                    dve.wait_ge(h_ready, t)
                V.tensor_scalar(flat(xn[:, :, :]), xt[:, b, :], stx[:, 0:1], None, ALU.mult).then_inc(xn_ready, 1)

            def modulate(t, fill0, cond):
                for f in range(2):
                    ks = slice(4 * f, 4 * f + 4)
                    dve.wait_ge(filled, fill0 + f + 1)
                    V.tensor_tensor(xn[:, ks, :], ps[:, TB + f, :].rearrange("p (k c) -> p k c", k=4),
                                    bc(mcol[:, 1, cond, ks], P), ALU.mult).then_inc(emptied, 1)
                dve.wait_ge(emptied, fill0 + 2)
                V.tensor_tensor(xn[:, :, :], xn[:, :, :], bc(mcol[:, 0, cond, :], P), ALU.add).then_inc(hv_ready, 1)
                dve.wait_ge(h_hi, t + 1)
                V.tensor_tensor(flat(hT[1][:, :, :]), flat(xn[:, :, :]), flat(hT[0][:, :, :]).bitcast(F32),
                                ALU.subtract).then_inc(h_ready, 1)

            def lo_fills(t):
                for k in range(7):
                    src = ps[:, TB + (k + 1) % 2, :]
                    dve.wait_ge(hi_ready, HI(t, k) + 1)
                    if k < 4:
                        x = (qT, kT)[k // 2]
                        hs = slice(4 * (k % 2), 4 * (k % 2) + 4)
                        ins = V.tensor_tensor(x[:, 1, hs, :].rearrange("p h c -> p (h c)"), src[0:QK, :],
                                              x[:, 0, hs, :].rearrange("p h c -> p (h c)").bitcast(F32), ALU.subtract)
                    elif k < 6:
                        hs = slice(4 * (k - 4), 4 * (k - 4) + 4)
                        for r in range(2):
                            hi, lo = (sT[SD * i:SD * i + SD, hs, :].rearrange("p (g r) c -> p r g c", r=2)[:, r] for i in range(2))
                            ins = V.tensor_tensor(lo, src[SD * r:SD * r + SD, 0:2 * P].rearrange("p (g c) -> p g c", g=2),
                                                  hi.bitcast(F32), ALU.subtract)
                    else:
                        ins = V.tensor_tensor(flat(sK[:, 1, :, :]), src[:, 0:SKV * P], flat(sK[:, 0, :, :]).bitcast(F32),
                                              ALU.subtract)
                    ins.then_inc(emptied, 1)

            def step(t, b, turn, cond=1):
                first = isinstance(t, int) and t == 0
                last = isinstance(t, int) and t == NT - 1
                if not last:
                    x_norm(EV(t, 0), t + 1, 1 - b)
                dve.wait_ge(squared, EV(t, 1) + 1)
                V.tensor_scalar(stc[:, 0:1], stc[:, 0:1], 1.0 / QL, EPS, ALU.mult, ALU.add)
                V.tensor_scalar(stc[:, 1:2], stc[:, 1:2], 1.0 / KVL, EPS, ALU.mult, ALU.add).then_inc(var_ready, 1)
                dve.wait_ge(root_ready, EV(t, 1) + 1)
                link(V.reciprocal(stc[:, :], stc[:, :]))
                V.scalar_tensor_tensor(out=flat(cn[:, 0:2, :]), in0=zs[:, 0:QL], scalar=stc[:, 0:1], in1=b_qa[:, :],
                                       op0=ALU.mult, op1=ALU.mult).then_inc(c_ready, 1)
                V.scalar_tensor_tensor(out=cn[:, 2, :], in0=zs[:, QL:384], scalar=stc[:, 1:2], in1=b_kva[:, :],
                                       op0=ALU.mult, op1=ALU.mult).then_inc(c_ready, 1)
                if not first:
                    lo_fills(t)
                if not last:
                    modulate(t + 1, FILL(t, 7), 1 if first else 0)
                dve.wait_ge(hi_ready, HI(t, 7) + 1)
                V.tensor_tensor(flat(cT[1][:, :, :]), ps[:, TB, 0:3 * P], flat(cT[0][:, :, :]).bitcast(F32),
                                ALU.subtract).then_inc(emptied, 1)
                dve.wait_ge(squared, EV(t, 2) + 1)
                V.tensor_reduce(stn[:, 16:26], sqs[:, :, :], AX.X, ALU.add)
                V.tensor_reduce(stn[:, 0:8], sqq[:, :, :], AX.X, ALU.add)
                link(V.tensor_reduce(stn[:, 8:16], sqk[:, :, :], AX.X, ALU.add))
                link(V.tensor_scalar(stn[:, 8:16], stn[:, 8:16], stn[:, 26:27], None, ALU.add))
                V.tensor_scalar(stn[:, 0:16], stn[:, 0:16], 1.0 / QK, EPS, ALU.mult, ALU.add)
                V.tensor_scalar(stn[:, 16:26], stn[:, 16:26], 1.0 / SD, EPS, ALU.mult, ALU.add).then_inc(var_ready, 1)
                dve.wait_ge(v_hi, t + 1)
                V.tensor_tensor(vm[:, :, VD:2 * VD], kv[:, :, NOPE:P], vm[:, :, 0:VD].bitcast(F32), ALU.subtract)
                V.tensor_tensor(vs[:, :, SD:2 * SD], zs[:, 1056:1184].rearrange("p (v d) -> p v d", v=SKV),
                                vs[:, :, 0:SD].bitcast(F32), ALU.subtract)
                dve.wait_ge(root_ready, EV(t, 2) + 1)
                link(V.reciprocal(stn[:, 0:26], stn[:, 0:26]))
                link(V.tensor_scalar(stn[:, 0:8], stn[:, 0:8], MLA_SCALE, None, ALU.mult))
                link(V.tensor_scalar(stn[:, 16:24], stn[:, 16:24], SWA_SCALE, None, ALU.mult))
                dve.wait_ge(gained, t + 1)
                tb = tab[:, b, :]
                V.tensor_tensor(ror[:, :, :], gr[:, :, :], mid(tb[:, 0:ROPE], 1), ALU.mult)
                V.tensor_tensor(roq[:, :, :], gq[:, :, NOPE:QK], mid(tb[:, 0:ROPE], HEADS), ALU.mult)
                link(V.tensor_tensor(ros[:, :, :], gs[:, :, :], mid(tb[:, 2 * ROPE:2 * ROPE + SD], NS), ALU.mult))
                V.tensor_tensor(ror[:, :, :], ror[:, :, :], swr[:, :, :], ALU.add)
                V.tensor_tensor(roq[:, :, :], roq[:, :, :], swq[:, :, :], ALU.add)
                link(V.tensor_tensor(ros[:, :, :], ros[:, :, :], sws[:, :, :], ALU.add))
                V.tensor_tensor(qn[:, :, 0:NOPE], gq[:, :, 0:NOPE], bc(stn[:, 0:8], NOPE), ALU.mult)
                V.tensor_tensor(qn[:, :, NOPE:QK], roq[:, :, :], bc(stn[:, 0:8], ROPE), ALU.mult)
                V.tensor_tensor(kn[:, :, 0:NOPE], gk[:, :, :], bc(stn[:, 8:16], NOPE), ALU.mult)
                V.tensor_tensor(kn[:, :, NOPE:QK], mid(ror[:, 0, :], HEADS), bc(stn[:, 8:16], ROPE), ALU.mult)
                V.tensor_tensor(sn[:, 0:SH, :], ros[:, 0:SH, :], bc(stn[:, 16:24], SD), ALU.mult)
                for r in range(2):
                    ins = V.tensor_tensor(sn[:, SH + r::2, :], ros[:, SH:NS, :], bc(stn[:, 24:26], SD), ALU.mult)
                ins.then_inc(normed, 1)

            dve.wait_ge(consts, 16 * 12)
            link(V.tensor_scalar_add(flat(mcol[:, 1, :, :]), flat(mcol[:, 1, :, :]), 1.0))
            link(V.tensor_tensor(mcol[:, 1, :, :], mcol[:, 1, :, :], mid(gcol[:, :], 2), ALU.mult))
            x_norm(0, 0, 0)
            modulate(0, 0, 1)
            step(0, 0, 0)
            step(1, 1, 0)
            with dve.Fori(1, NT // 2 - 1) as i:
                link.enter(i - 1, 18)
                step(i * 2, 0, i)
                step(i * 2 + 1, 1, i)
                link.leave(NT // 2 - 2)
            step(NT - 2, 0, NT // 2 - 1)
            step(NT - 1, 1, NT // 2 - 1)
            lo_fills(NT)

        @block.tensor
        def _(pe):
            MM = nc.tensor.matmul

            def fill(n, bank, parts):
                if not (isinstance(n, int) and n < 2):
                    pe.wait_ge(emptied, n - 1)
                at = 0
                for x in parts:
                    m = x.shape[1]
                    last = nc.tensor.transpose(ps[0:m, TB + bank, at:at + P], x, ident[:, :])
                    at += P
                last.then_inc(filled, 1)

            def fill_x(n):
                for f in range(2):
                    fill(n + f, f, [xn[:, k, :] for k in range(4 * f, 4 * f + 4)])

            def fills(t):
                pe.wait_ge(normed, t)
                for k in range(7):
                    if k < 4:
                        h0 = 4 * (k % 2)
                        parts = [(qn, kn)[k // 2][:, h, :] for h in range(h0, h0 + 4)]
                    else:
                        parts = [flat(sn[:, h:h + 2, :]) for h in (4 * (k - 4), 4 * (k - 4) + 2)]
                    fill(FILL(t, k), (k + 1) % 2, parts)

            def step(t, b):
                first = isinstance(t, int) and t == 0
                last = isinstance(t, int) and t == NT - 1
                pe.wait_ge(h_ready, t + 1)
                for j, (lo, hi) in enumerate(ZCH):
                    if not first:
                        pe.wait_ge(z_copied, t * 3 + j - 2)
                    for k in range(KC):
                        for i, (a, w) in enumerate(((0, 0), (0, 1), (1, 0))):
                            ins = MM(ps[:, j, 0:hi - lo], hT[a][:, k, :], w_in[w][:, k, lo:hi],
                                     start=(k == 0 and i == 0), stop=(k == KC - 1 and i == 2))
                    ins.then_inc(z_ready, 1)
                if not first:
                    fills(t)
                if not last:
                    pe.wait_ge(xn_ready, t + 2)
                    fill_x(FILL(t, 7))
                pe.wait_ge(c_ready, t * 2 + 2)
                fill(FILL(t, 9), 0, [cn[:, i, :] for i in range(3)])
                pe.wait_ge(emptied, FILL(t, 9) + 1)
                for j in range(4):
                    bank = (0, 1, 2, 0)[j]
                    if j == 3:
                        pe.wait_ge(u_copied, t * 4 + 1)
                    elif not first:
                        pe.wait_ge(u_copied, t * 4 + (0, -2, -1)[j])
                    if j < 2:
                        for k in range(2):
                            for i, (a, w) in enumerate(((0, 0), (0, 1), (1, 0))):
                                ins = MM(ps[:, UB + bank, 0:4 * QK], cT[a][:, k, :], w_uq[w][:, k, j * 4 * QK:(j + 1) * 4 * QK],
                                         start=(k == 0 and i == 0), stop=(k == 1 and i == 2))
                    else:
                        for i, (a, w) in enumerate(((0, 0), (0, 1), (1, 0))):
                            ins = MM(ps[:, UB + bank, :], cT[a][:, 2, :], w_kv[w][:, (j - 2) * BANK:(j - 1) * BANK],
                                     start=(i == 0), stop=(i == 2))
                    ins.then_inc(u_ready, 1)

            pe.wait_ge(consts, 16 * 12)
            pe.wait_ge(xn_ready, 1)
            fill_x(0)
            for t in range(2):
                step(t, t)
            with pe.Fori(1, NT // 2 - 1) as i:
                step(i * 2, 0)
                step(i * 2 + 1, 1)
            step(NT - 2, 0)
            step(NT - 1, 1)
            fills(NT)


def swa_phase(nc, A, scr, mix, rs):
    with ExitStack() as ctx:
        sb = lambda n, s, d=F32: ctx.enter_context(nc.sbuf_tensor(n, s, d))
        sem = lambda n: ctx.enter_context(nc.semaphore(n))
        NKEY = UNITK * P
        ident = sb("s_ident", [P, P])
        sink = sb("s_sink", [P, SH])
        mask = sb("s_mask", [P, 2, CTX + 3 * P + CTX])
        qs = sb("s_q", [P, 2, GRP * P], F32R)
        kb = sb("s_k", [P, 2, 2, NKEY], F32R)
        vb = sb("s_v", [P, 2, UNITK, 2 * SD], F32R)
        sc = sb("s_sc", [P, 2, NKEY])
        pr = sb("s_pr", [P, 2, 2, NKEY])
        pT = [sb(f"s_pT{i}", [P, 2, UNITK, GRP, P], F32R) for i in range(2)]
        ot = sb("s_ot", [SD, 2, GRP * P])
        mx = sb("s_mx", [P, 2])
        nb = sb("s_nb", [P, 2])
        ds = sb("s_ds", [P, 2])
        se = sb("s_se", [P, 2])
        sm = sb("s_sm", [P, 2])
        ps = ctx.enter_context(nc.psum_tensor("s_ps", [P, 8, BANK], F32))
        TB, OB = 3, 6
        consts = sem("s_consts")
        cleared = sem("s_cleared")
        loaded = [sem(f"s_loaded{i}") for i in range(2)]
        scored = sem("s_scored")
        masked = sem("s_masked")
        shift_ready = sem("s_shift_ready")
        exped = sem("s_exped")
        filled = sem("s_filled")
        hi_ready = sem("s_hi_ready")
        emptied = sem("s_emptied")
        out_ready = sem("s_out_ready")
        out_low = sem("s_out_low")
        out_done = sem("s_out_done")
        v_chain = sem("s_v_chain")
        block = ctx.enter_context(nc.Block())
        NU = SKV * NB
        UPI = 2 * SKV

        def tile_at(hh, kt):
            return P * (kt if hh == 1 else (kt + 3 if kt < 2 else kt - 2))

        FILLS = (((0, 0, 4, 0),), ((1, 0, 4, 0),), ((0, 4, 1, 0), (1, 4, 1, P)))

        @block.sync
        def _(sp):
            def load(j, u, n, wait=True):
                kv, blk, b = u // 2, j * 2 + u % 2, u % 2
                if wait:
                    sp.wait_ge(out_ready, n - 1)
                col = blk * P
                sp.dma_start(qs[:, b, :].bitcast(F32), scr["sq"][bass.ds(blk + NCT, 1), :, kv * GRP * P:(kv + 1) * GRP * P]
                             .rearrange("a p c -> p (a c)")).then_inc(loaded[b], 16)
                sp.dma_start(kb[:, b, :, 0:CTX].bitcast(F32),
                             scr["sk"][kv, :, :, 0:CTX].rearrange("i p c -> p i c")).then_inc(loaded[b], 16)
                sp.dma_start(kb[:, b, :, CTX:NKEY].bitcast(F32),
                             scr["sk"][kv, :, :, bass.ds(col + CTX, 3 * P)].rearrange("i p c -> p i c")).then_inc(loaded[b], 16)
                sp.dma_start(vb[:, b, 0:NCT, :].bitcast(F32),
                             scr["sv"][0:NCT, :, kv * P:(kv + 1) * P].rearrange("a p c -> p a c")).then_inc(loaded[b], 16)
                sp.dma_start(vb[:, b, NCT:UNITK, :].bitcast(F32),
                             scr["sv"][bass.ds(blk + NCT, 3), :, kv * P:(kv + 1) * P].rearrange("a p c -> p a c")).then_inc(loaded[b], 16)
                sp.dma_start(mask[:, b, CTX:CTX + 3 * P],
                             A["mask"][bass.ds(blk, 1)].rearrange("a p c -> p (a c)")).then_inc(loaded[b], 16)

            sp.dma_start(ident[:, :], A["ident"]).then_inc(consts, 16)
            sp.dma_start(sink[:, :], A["swa_sink"].partition_broadcast(P).rearrange("p a n -> p (a n)")).then_inc(consts, 16)
            for u in range(UPI):
                load(0, u, u, wait=u >= 2)
            with sp.Fori(1, NB // 2) as j:
                for u in range(UPI):
                    load(j, u, j * UPI + u)

        @block.gpsimd
        def _(pool):
            for b in range(2):
                nc.gpsimd.memset(mask[:, b, 0:CTX], 0.0).then_inc(cleared, 1)
                nc.gpsimd.memset(mask[:, b, CTX + 3 * P:], 0.0).then_inc(cleared, 1)

        @block.scalar
        def _(act):
            def hi_fill(s, k, kind):
                n = s * 3 + k
                act.wait_ge(filled, n + 1)
                pair, ub = kind % 2, (kind // 2) % 2
                for hh, kt0, nk, at in FILLS[k]:
                    ins = nc.scalar.activation(pT[0][:, ub, kt0:kt0 + nk, 2 * pair + hh, :],
                                               ps[:, TB + k, at:at + nk * P].rearrange("p (k c) -> p k c", k=nk), ACT.Copy)
                ins.then_inc(hi_ready, 1)

            def out_low_copy(n, b):
                act.wait_ge(out_ready, n + 1)
                nc.scalar.activation(ot[:, b, :], ps[SD:P, OB + b, :], ACT.Copy).then_inc(out_low, 1)

            def step(s, kind, head=True, tail=True, lag=True):
                if tail:
                    if (kind - 1) % 2 == 0 and lag:
                        act.wait_ge(out_ready, (s - 1) // 2 - 1 if isinstance(s, int) else s_half(s, kind) - 1)
                    for k in range(3):
                        hi_fill(s - 1, k, kind - 1)
                if head:
                    act.wait_ge(shift_ready, s + 1)
                    nc.scalar.activation(se[:, :], ds[:, :], ACT.Exp)
                    for hh in range(2):
                        ins = nc.scalar.activation(pr[:, kind % 2, hh, :], sc[:, hh, :], ACT.Exp, bias=nb[:, hh:hh + 1],
                                                   accum_out=sm[:, hh:hh + 1])
                    ins.then_inc(exped, 1)

            def s_half(s, kind):
                return base_unit[0] + (kind - 1) // 2

            base_unit = [0]
            act.wait_ge(cleared, 4)
            SPI = 2 * UPI
            for kind in range(SPI):
                s = kind
                step(s, kind, tail=s > 0, lag=(s - 1) // 2 >= 2)
                if s >= 3 and s % 2 == 1:
                    out_low_copy((s - 3) // 2, ((s - 3) // 2) % 2)
            with act.Fori(1, NB // 2) as j:
                base_unit[0] = j * UPI
                for kind in range(SPI):
                    step(j * SPI + kind, kind)
                    if kind % 2 == 1:
                        out_low_copy(j * UPI + (kind - 3) // 2, ((kind - 3) // 2) % 2)
            S = 2 * NU
            step(S, 0, head=False)
            out_low_copy(NU - 1, 1)

        @block.vector
        def _(dve):
            V = nc.vector
            link = Chain(dve, v_chain)

            def out(n, b, kv, blk):
                dve.wait_ge(out_low, n + 1)
                for r in range(2):
                    c0 = 4 + 2 * kv
                    V_ = V.tensor_tensor(mix[SD * r:SD * r + SD, c0:c0 + 2, bass.ds(blk * P, P)],
                                         ps[0:SD, OB + b, :].rearrange("p (g r c) -> p r g c", r=2, c=P)[:, r, :, :],
                                         ot[:, b, :].rearrange("p (g r c) -> p r g c", r=2, c=P)[:, r, :, :], ALU.add)
                V_.then_inc(out_done, 1)

            def lo_fill(s, k, kind):
                n = s * 3 + k
                pair, ub = kind % 2, (kind // 2) % 2
                dve.wait_ge(hi_ready, n + 1)
                for hh, kt0, nk, at in FILLS[k]:
                    ins = V.tensor_tensor(pT[1][:, ub, kt0:kt0 + nk, 2 * pair + hh, :],
                                          ps[:, TB + k, at:at + nk * P].rearrange("p (k c) -> p k c", k=nk),
                                          pT[0][:, ub, kt0:kt0 + nk, 2 * pair + hh, :].bitcast(F32), ALU.subtract)
                ins.then_inc(emptied, 1)

            def head(s, kind, blk):
                kv, pair, b = (kind // 4) % 2, kind % 2, (kind // 2) % 2
                h0 = kv * GRP + 2 * pair
                for hh in range(2):
                    dve.wait_ge(scored, s * 2 + 2)
                    m = mask[:, b, CTX:] if hh == 0 else mask[:, b, 0:NKEY]
                    src = ps[:, 0:3, :].rearrange("p a b -> p (a b)")[:, P + hh * NKEY:P + (hh + 1) * NKEY]
                    V.tensor_tensor(sc[:, hh, :], src, m, ALU.add).then_inc(masked, 1)
                    dve.wait_ge(masked, s * 2 + hh + 1)
                    ins = V.reduce_max(mx[:, hh:hh + 1], sc[:, hh, :], AX.X)
                link(ins)
                link(V.tensor_tensor(mx[:, :], mx[:, :], sink[:, h0:h0 + 2], ALU.max))
                V.tensor_scalar(nb[:, :], mx[:, :], -1.0, None, ALU.mult)
                V.tensor_tensor(ds[:, :], sink[:, h0:h0 + 2], mx[:, :], ALU.subtract).then_inc(shift_ready, 1)

            def sums(s, kind, blk):
                kv, pair = (kind // 4) % 2, kind % 2
                h0 = kv * GRP + 2 * pair
                dve.wait_ge(exped, s + 1)
                link(V.tensor_tensor(sm[:, :], sm[:, :], se[:, :], ALU.add))
                link(V.reciprocal(sm[:, :], sm[:, :]))
                link(V.tensor_scalar(rs[:, bass.ds(blk, 1), HEADS + h0:HEADS + h0 + 2].rearrange("p a b -> p (a b)"),
                                     sm[:, :], 1.0, None, ALU.mult))

            def body(j, s0, kinds, first):
                for kind in kinds:
                    s, blk = s0 + kind, j * 2 + (kind // 2) % 2
                    if kind == 0:
                        pkind, pblk, pj = 7, j * 2 - 1, j
                    else:
                        pkind, pblk = kind - 1, j * 2 + ((kind - 1) // 2) % 2
                    has_prev = not (first and kind == 0)
                    if has_prev:
                        sums(s - 1, pkind, pblk)
                    head(s, kind, blk)
                    if has_prev:
                        for k in range(3):
                            lo_fill(s - 1, k, pkind)
                    if kind % 2 == 1 and not (first and kind < 3):
                        un = (kind - 3) // 2
                        if un >= 0:
                            out(s0 // 2 + un if isinstance(s0, int) else j * UPI + un, un % 2, un // 2, j * 2 + un % 2)
                        else:
                            out(j * UPI - 1, 1, 1, j * 2 - 1)

            dve.wait_ge(consts, 32)
            dve.wait_ge(cleared, 4)
            SPI = 2 * UPI
            body(0, 0, range(SPI), True)
            with dve.Fori(1, NB // 2) as j:
                link.enter(j - 1, 5 * SPI)
                body(j, j * SPI, range(SPI), False)
                link.leave(NB // 2 - 1)
            S, last = 2 * NU, NB // 2
            sums(S - 1, 7, NB - 1)
            for k in range(3):
                lo_fill(S - 1, k, 7)
            out(NU - 1, 1, 1, NB - 1)

        @block.tensor
        def _(pe):
            def scores(s, kind, n, turn, wait):
                b, pair = (kind // 2) % 2, kind % 2
                flat_ps = ps[:, 0:3, :].rearrange("p a b -> p (a b)")
                if pair == 0:
                    pe.wait_ge(loaded[b], turn * 96 + 96)
                if wait:
                    pe.wait_ge(masked, s * 2)
                for hh in range(2):
                    q = qs[:, b, (2 * pair + hh) * P:(2 * pair + hh + 1) * P]
                    base = P + hh * NKEY
                    ctx_at, band_at = (base + 3 * P, base) if hh == 0 else (base, base + CTX)
                    for at, lo, hi in ((band_at, CTX, NKEY), (ctx_at, 0, CTX)):
                        for i in range(2):
                            ins = nc.tensor.matmul(flat_ps[:, at:at + hi - lo], q, kb[:, b, i, lo:hi],
                                                   start=(i == 0), stop=(i == 1))
                    ins.then_inc(scored, 1)

            def transposes(s, kind, wait):
                pe.wait_ge(exped, s + 1)
                for k in range(3):
                    if wait:
                        pe.wait_ge(emptied, s * 3 + k - 2)
                    for hh, kt0, nk, at in FILLS[k]:
                        for kt in range(kt0, kt0 + nk):
                            c = tile_at(hh, kt)
                            last = nc.tensor.transpose(ps[:, TB + k, at + (kt - kt0) * P:at + (kt - kt0 + 1) * P],
                                                       pr[:, kind % 2, hh, c:c + P], ident[:, :])
                    last.then_inc(filled, 1)

            def values(n, ub, s_end, wait):
                pe.wait_ge(emptied, s_end)
                if wait:
                    pe.wait_ge(out_done, n - 1)
                for kt in range(UNITK):
                    for i in range(2):
                        last = nc.tensor.matmul(ps[:, OB + ub, :], vb[:, ub, kt, :], pT[i][:, ub, kt, :, :].rearrange("p g c -> p (g c)"),
                                                start=(kt == 0 and i == 0), stop=(kt == UNITK - 1 and i == 1))
                last.then_inc(out_ready, 1)

            SPI = 2 * UPI

            def body(j, s0, turn0, first):
                for kind in range(SPI):
                    s = s0 + kind
                    turn = turn0 + kind // 4
                    scores(s, kind, None, turn, not (first and kind == 0))
                    if not (first and kind == 0):
                        transposes(s - 1, (kind - 1) % SPI, not (first and kind == 1))
                    if kind % 2 == 1 and not (first and kind == 1):
                        un = (kind - 3) // 2
                        n = (s0 // 2 if isinstance(s0, int) else j * UPI) + un
                        values(n, un % 2, n * 6 + 6, not (first and un < 2))

            pe.wait_ge(consts, 32)
            body(0, 0, 0, True)
            with pe.Fori(1, NB // 2) as j:
                body(j, j * SPI, j * 2, False)
            S = 2 * NU
            transposes(S - 1, 7, True)
            values(NU - 1, 1, NU * 6, True)


def mla_phase(nc, A, scr, mix, rs):
    with ExitStack() as ctx:
        sb = lambda n, s, d=F32: ctx.enter_context(nc.sbuf_tensor(n, s, d))
        sem = lambda n: ctx.enter_context(nc.semaphore(n))
        ident = sb("l_ident", [P, P])
        qT = sb("l_q", [QK, 2, 2, SEQ], F32R)
        kT = sb("l_k", [QK, 2, 2, KALL], F32R)
        vb = sb("l_v", [P, 2, NT, 2 * VD], F32R)
        pr = sb("l_pr", [P, 2, KALL])
        pT = [sb(f"l_pT{i}", [P, 2, NT, 2, P], F32R) for i in range(2)]
        ot = sb("l_ot", [VD, 2 * P])
        nb = sb("l_nb", [P, 2])
        sm = sb("l_sm", [P, 2])
        inv = sb("l_inv", [P, 1])
        ps = ctx.enter_context(nc.psum_tensor("l_ps", [P, 8, BANK], F32))
        fps = ps[:, 0:5, :].rearrange("p a b -> p (a b)")
        TB, OB = 5, 7
        consts = sem("l_consts")
        loaded = [sem(f"l_loaded{i}") for i in range(2)]
        scored = sem("l_scored")
        shift_ready = sem("l_shift_ready")
        exped = sem("l_exped")
        filled = sem("l_filled")
        hi_ready = sem("l_hi_ready")
        emptied = sem("l_emptied")
        out_ready = sem("l_out_ready")
        out_low = sem("l_out_low")
        out_done = sem("l_out_done")
        v_chain = sem("l_v_chain")
        block = ctx.enter_context(nc.Block())
        TILES = ((0, 4), (4, 8), (8, 10))
        SPI = 2 * NB
        TURNS = HEADS // 2
        S = HEADS * NB

        @block.sync
        def _(sp):
            def load(h, b):
                sp.dma_start(qT[:, b, :, :].bitcast(F32), scr["q"][bass.ds(h, 1), :, :, CTX:KALL]
                             .rearrange("a p i c -> p (a i) c")).then_inc(loaded[b], 16)
                sp.dma_start(kT[:, b, :, :].bitcast(F32), scr["k"][bass.ds(h, 1)]
                             .rearrange("a p i c -> p (a i) c")).then_inc(loaded[b], 16)
                sp.dma_start(vb[:, b, :, :].bitcast(F32), scr["v"][bass.ds(h, 1)]
                             .rearrange("a t p c -> p (a t) c")).then_inc(loaded[b], 16)

            sp.dma_start(ident[:, :], A["ident"]).then_inc(consts, 16)
            load(0, 0)
            load(1, 1)
            with sp.Fori(1, TURNS) as j:
                for b in range(2):
                    sp.wait_ge(out_ready, j * 8 - 4 + 4 * b)
                    load(j * 2 + b, b)

        @block.tensor
        def _(pe):
            def scores(s, kind, j, wait):
                b, qt = kind // NB, kind % NB
                if qt == 0:
                    pe.wait_ge(loaded[b], j * 48 + 48)
                if wait:
                    pe.wait_ge(exped, s - 1)
                even = kind % 2 == 0
                chunks = ((0, 0, 512), (512, 512, 1024), (1024, 1024, 1280)) if even else \
                    ((1536, 256, 768), (2048, 768, 1280), (1280, 0, 256))
                for c, (at, lo, hi) in enumerate(chunks):
                    if c == 2 and (wait or kind == 1):
                        pe.wait_ge(exped, s)
                    for i, (a, w) in enumerate(((0, 0), (0, 1), (1, 0))):
                        last = nc.tensor.matmul(fps[:, at:at + hi - lo], qT[:, b, a, qt * P:(qt + 1) * P],
                                                kT[:, b, w, lo:hi], start=(i == 0), stop=(i == 2))
                last.then_inc(scored, 1)

            def fill(s, kind, k, wait):
                n_par = (kind * 3 + k) % 2
                if k == 0:
                    pe.wait_ge(exped, s + 1)
                if wait:
                    pe.wait_ge(emptied, s * 3 + k - 1)
                lo, hi = TILES[k]
                for t in range(lo, hi):
                    last = nc.tensor.transpose(ps[:, TB + n_par, (t - lo) * P:(t - lo + 1) * P],
                                               pr[:, kind % 2, t * P:(t + 1) * P], ident[:, :])
                last.then_inc(filled, 1)

            def values(u, ukind, half, wait):
                b, ub = (ukind // 4) % 2, ukind % 2
                if half == 0:
                    pe.wait_ge(emptied, u * 6 + 6)
                    if wait:
                        pe.wait_ge(out_done, u)
                for t in range(NT):
                    last = nc.tensor.matmul(ps[:, OB, 0:2 * P], vb[:, b, t, :],
                                            pT[half][:, ub, t, :, :].rearrange("p q c -> p (q c)"),
                                            start=(half == 0 and t == 0), stop=(half == 1 and t == NT - 1))
                if half == 1:
                    last.then_inc(out_ready, 1)

            def turn(j, s0, u0, first):
                for kind in range(SPI):
                    s = s0 + kind
                    scores(s, kind, j, not (first and kind < 2))
                    prev = (kind - 1) % SPI
                    if not (first and kind == 0):
                        for k in range(2):
                            fill(s - 1, prev, k, not (first and kind == 1))
                    if not (first and kind < 3):
                        uk = (kind - 3) // 2
                        half = 0 if kind % 2 == 1 else 1
                        values(u0 + uk, uk % 8, half, not (first and uk == 0))
                    if not (first and kind == 0):
                        fill(s - 1, prev, 2, True)

            pe.wait_ge(consts, 16)
            turn(0, 0, 0, True)
            with pe.Fori(1, TURNS) as j:
                turn(j, j * SPI, j * 8, False)
            for k in range(2):
                fill(S - 1, SPI - 1, k, True)
            values(S // 2 - 2, 6, 1, True)
            fill(S - 1, SPI - 1, 2, True)
            values(S // 2 - 1, 7, 0, True)
            values(S // 2 - 1, 7, 1, True)

        @block.scalar
        def _(act):
            def hi_fill(s, kind, k):
                n_par = (kind * 3 + k) % 2
                ub, q2 = (kind // 2) % 2, kind % 2
                lo, hi = TILES[k]
                act.wait_ge(filled, s * 3 + k + 1)
                nc.scalar.activation(pT[0][:, ub, lo:hi, q2, :],
                                     ps[:, TB + n_par, 0:(hi - lo) * P].rearrange("p (t c) -> p t c", c=P),
                                     ACT.Copy).then_inc(hi_ready, 1)

            def turn(s0, u0, first):
                for kind in range(SPI):
                    s = s0 + kind
                    prev = (kind - 1) % SPI
                    if not (first and kind == 0):
                        if prev % 2 == 0 and not (first and kind < 5):
                            act.wait_ge(out_ready, u0 + (kind - 1) // 2 - 1)
                        for k in range(2):
                            hi_fill(s - 1, prev, k)
                    act.wait_ge(shift_ready, s + 1)
                    nc.scalar.activation(pr[:, kind % 2, :], fps[:, (kind % 2) * KALL:(kind % 2 + 1) * KALL], ACT.Exp,
                                         bias=nb[:, kind % 2:kind % 2 + 1],
                                         accum_out=sm[:, kind % 2:kind % 2 + 1]).then_inc(exped, 1)
                    if not (first and kind == 0):
                        hi_fill(s - 1, prev, 2)
                    if kind % 2 == 0 and not (first and kind < 4):
                        low(u0 + (kind - 4) // 2)

            def low(u):
                act.wait_ge(out_ready, u + 1)
                nc.scalar.activation(ot[:, :], ps[VD:P, OB, 0:2 * P], ACT.Copy).then_inc(out_low, 1)

            turn(0, 0, True)
            with act.Fori(1, TURNS) as j:
                turn(j * SPI, j * 8, False)
            for k in range(3):
                hi_fill(S - 1, SPI - 1, k)
            low(S // 2 - 2)
            low(S // 2 - 1)

        @block.vector
        def _(dve):
            V = nc.vector
            link = Chain(dve, v_chain)

            def lo_fill(s, kind, k):
                n_par = (kind * 3 + k) % 2
                ub, q2 = (kind // 2) % 2, kind % 2
                lo, hi = TILES[k]
                dve.wait_ge(hi_ready, s * 3 + k + 1)
                V.tensor_tensor(pT[1][:, ub, lo:hi, q2, :],
                                ps[:, TB + n_par, 0:(hi - lo) * P].rearrange("p (t c) -> p t c", c=P),
                                pT[0][:, ub, lo:hi, q2, :].bitcast(F32), ALU.subtract).then_inc(emptied, 1)

            def out(u, h, uk):
                r, q0 = (uk // 4) % 2, (uk % 4) * 2 * P
                dve.wait_ge(out_low, u + 1)
                V.tensor_tensor(mix[VD * r:VD * r + VD, bass.ds(h, 1), q0:q0 + 2 * P].rearrange("p a c -> p (a c)"),
                                ps[0:VD, OB, 0:2 * P], ot[:, :], ALU.add).then_inc(out_done, 1)

            def total(s, kind, j):
                dve.wait_ge(exped, s + 1)
                link(V.reciprocal(inv[:, :], sm[:, kind % 2:kind % 2 + 1]))
                V.tensor_scalar(rs[:, kind % NB, bass.ds(j * 2 + kind // NB, 1)], inv[:, :], 1.0, None, ALU.mult)

            def turn(j, s0, u0, first):
                for kind in range(SPI):
                    s = s0 + kind
                    prev = (kind - 1) % SPI
                    pj = j - 1 if kind == 0 else j
                    dve.wait_ge(scored, s + 1)
                    V.tensor_reduce(nb[:, kind % 2:kind % 2 + 1], fps[:, (kind % 2) * KALL:(kind % 2 + 1) * KALL],
                                    AX.X, ALU.max, negate=True).then_inc(shift_ready, 1)
                    if not (first and kind == 0):
                        total(s - 1, prev, pj)
                        for k in range(3):
                            lo_fill(s - 1, prev, k)
                    if kind % 2 == 0 and not (first and kind < 4):
                        uk = (kind - 4) // 2
                        out(u0 + uk, j - 1 if uk < 0 else j, uk % 8)

            turn(0, 0, 0, True)
            with dve.Fori(1, TURNS) as j:
                link.enter(j - 1, SPI)
                turn(j, j * SPI, j * 8, False)
                link.leave(TURNS - 1)
            total(S - 1, SPI - 1, TURNS - 1)
            for k in range(3):
                lo_fill(S - 1, SPI - 1, k)
            out(S // 2 - 2, TURNS - 1, 6)
            out(S // 2 - 1, TURNS - 1, 7)


def out_phase(nc, A, scr, mix, rs, h2):
    with ExitStack() as ctx:
        sb = lambda n, s, d=F32: ctx.enter_context(nc.sbuf_tensor(n, s, d))
        sem = lambda n: ctx.enter_context(nc.semaphore(n))
        WR = 2
        w_out = [sb(f"o_w{i}", [P, KC, D], F32R) for i in range(2)]
        raw = sb("o_raw", [P, WR, D])
        ident = sb("o_ident", [P, P])
        g1 = sb("o_g1", [P, D])
        mcol = sb("o_mcol", [P, 2, KC])
        gcol = sb("o_gcol", [P, KC])
        rb = sb("o_rb", [P, HEADS + SH, VD])
        mn = sb("o_mn", [P, KC, P])
        mT = [sb(f"o_m{i}", [P, KC, P], F32R) for i in range(2)]
        xt = sb("o_x", [P, D])
        x1 = sb("o_x1", [P, D])
        xn = sb("o_xn", [P, KC, P])
        st = sb("o_st", [P, 1])
        ps = ctx.enter_context(nc.psum_tensor("o_ps", [P, 8, BANK], F32))
        BB, YB, TB = 0, 2, 4
        consts = sem("o_consts")
        w_loaded = [sem(f"o_w_loaded{i}") for i in range(WR)]
        w_hi = sem("o_w_hi")
        w_lo = sem("o_w_lo")
        x_loaded = sem("o_x_loaded")
        widened = sem("o_widened")
        spread = sem("o_spread")
        scaled = sem("o_scaled")
        m_hi = sem("o_m_hi")
        m_ready = sem("o_m_ready")
        y_ready = sem("o_y_ready")
        gated = sem("o_gated")
        x1_ready = sem("o_x1_ready")
        squared = sem("o_squared")
        var_ready = sem("o_var_ready")
        root_ready = sem("o_root_ready")
        xn_ready = sem("o_xn_ready")
        turned = sem("o_turned")
        scaled_h = sem("o_scaled_h")
        hv_ready = sem("o_hv_ready")
        h_hi = sem("o_h_hi")
        h_ready = sem("o_h_ready")
        stored = sem("o_stored")
        v_chain = sem("o_v_chain")
        block = ctx.enter_context(nc.Block())

        @block.sync
        def _(sp):
            sp.dma_start(ident[:, :], A["ident"]).then_inc(consts, 16)
            sp.dma_start(g1[:, :], scr["mod"][0:1, 2 * D:3 * D].partition_broadcast(P).rearrange("p a n -> p (a n)")).then_inc(consts, 16)
            with nc.allow_non_contiguous_dma(reason="a few vectors, one element a row"):
                sp.dma_start(gcol[:, :], A["g_mlp"].rearrange("l (k p) -> p (l k)", p=P)).then_inc(consts, 16)
                for s in range(2):
                    sp.dma_start(mcol[:, s, :],
                                 scr["mod"][0, (3 + s) * D:(4 + s) * D].rearrange("(k p) -> p k", p=P)).then_inc(consts, 16)
            for k in range(KC):
                if k >= WR:
                    sp.wait_ge(w_lo, k - WR + 1)
                sp.dma_start(raw[:, k % WR, :], A["w_out"][0, k * P:(k + 1) * P, :]).then_inc(w_loaded[k % WR], 16)
            for t in range(NB):
                if t:
                    sp.wait_ge(x1_ready, t)
                sp.dma_start(xt[:, :], A["x"][0, t * P:(t + 1) * P, :]).then_inc(x_loaded, 16)
                if t:
                    sp.dma_start(scr["x1"][(t - 1) * P:t * P, :], x1[:, :]).then_inc(stored, 16)
            sp.wait_ge(x1_ready, NB)
            sp.dma_start(scr["x1"][(NB - 1) * P:, :], x1[:, :]).then_inc(stored, 16)
            sp.wait_ge(stored, 16 * NB)

        @block.gpsimd
        def _(pool):
            for t in range(NB):
                if t:
                    pool.wait_ge(spread, 2 * t)
                nc.gpsimd.tensor_copy(rb[:, :, :], bc(rs[:, t, :], VD)).then_inc(widened, 1)

        @block.scalar
        def _(act):
            for k in range(KC):
                act.wait_ge(w_loaded[k % WR], 16 * (k // WR + 1))
                nc.scalar.activation(w_out[0][:, k, :], raw[:, k % WR, :], ACT.Copy).then_inc(w_hi, 1)

            def high_mix(t):
                act.wait_ge(scaled, 2 * t + 2)
                if t:
                    act.wait_ge(y_ready, 2 * t)
                nc.scalar.activation(flat(mT[0][:, :, :]), flat(mn[:, :, :]), ACT.Copy).then_inc(m_hi, 1)

            high_mix(0)
            for t in range(NB):
                if t + 1 < NB:
                    high_mix(t + 1)
                act.wait_ge(x1_ready, t + 1)
                if t:
                    act.wait_ge(turned, 2 * t)
                nc.scalar.activation(flat(xn[:, :, :]), x1[:, :], ACT.Square, accum_out=st[:, :]).then_inc(squared, 1)
                act.wait_ge(var_ready, t + 1)
                nc.scalar.activation(st[:, :], st[:, :], ACT.Sqrt).then_inc(root_ready, 1)
                act.wait_ge(hv_ready, t + 1)
                nc.scalar.activation(h2[0][:, :, t * P:(t + 1) * P], xn[:, :, :], ACT.Copy).then_inc(h_hi, 1)

        @block.vector
        def _(dve):
            V = nc.vector
            link = Chain(dve, v_chain)
            for k in range(KC):
                dve.wait_ge(w_hi, k + 1)
                V.tensor_tensor(w_out[1][:, k, :], raw[:, k % WR, :], w_out[0][:, k, :].bitcast(F32),
                                ALU.subtract).then_inc(w_lo, 1)
            dve.wait_ge(consts, 16 * 5)
            link(V.tensor_scalar_add(mcol[:, 1, :], mcol[:, 1, :], 1.0))
            link(V.tensor_tensor(mcol[:, 1, :], mcol[:, 1, :], gcol[:, :], ALU.mult))

            def scale_mix(t):
                if t:
                    dve.wait_ge(m_ready, t)
                for f in range(2):
                    dve.wait_ge(spread, 2 * t + f + 1)
                    V.tensor_tensor(mn[:, 4 * f:4 * f + 4, :], ps[:, BB + f, :].rearrange("p (k c) -> p k c", k=4),
                                    mix[:, 4 * f:4 * f + 4, t * P:(t + 1) * P], ALU.mult).then_inc(scaled, 1)

            def low_mix(t):
                dve.wait_ge(m_hi, t + 1)
                V.tensor_tensor(flat(mT[1][:, :, :]), flat(mn[:, :, :]), flat(mT[0][:, :, :]).bitcast(F32),
                                ALU.subtract).then_inc(m_ready, 1)

            scale_mix(0)
            low_mix(0)
            for t in range(NB):
                if t + 1 < NB:
                    scale_mix(t + 1)
                    low_mix(t + 1)
                dve.wait_ge(y_ready, 2 * t + 2)
                if t:
                    dve.wait_ge(stored, 16 * t)
                V.tensor_tensor(x1[:, :], flat(ps[:, YB:YB + 2, :]), g1[:, :], ALU.mult).then_inc(gated, 1)
                dve.wait_ge(gated, t + 1)
                dve.wait_ge(x_loaded, 16 * t + 16)
                V.tensor_tensor(x1[:, :], x1[:, :], xt[:, :], ALU.add).then_inc(x1_ready, 1)
                dve.wait_ge(squared, t + 1)
                V.tensor_scalar(st[:, :], st[:, :], 1.0 / D, EPS, ALU.mult, ALU.add).then_inc(var_ready, 1)
                dve.wait_ge(root_ready, t + 1)
                link(V.reciprocal(st[:, :], st[:, :]))
                V.tensor_scalar(flat(xn[:, :, :]), x1[:, :], st[:, 0:1], None, ALU.mult).then_inc(xn_ready, 1)
                for f in range(2):
                    dve.wait_ge(turned, 2 * t + f + 1)
                    V.tensor_tensor(xn[:, 4 * f:4 * f + 4, :], ps[:, TB + f, :].rearrange("p (k c) -> p k c", k=4),
                                    bc(mcol[:, 1, 4 * f:4 * f + 4], P), ALU.mult).then_inc(scaled_h, 1)
                dve.wait_ge(scaled_h, 2 * t + 2)
                V.tensor_tensor(xn[:, :, :], xn[:, :, :], bc(mcol[:, 0, :], P), ALU.add).then_inc(hv_ready, 1)
                dve.wait_ge(h_hi, t + 1)
                V.tensor_tensor(h2[1][:, :, t * P:(t + 1) * P], xn[:, :, :], h2[0][:, :, t * P:(t + 1) * P].bitcast(F32),
                                ALU.subtract).then_inc(h_ready, 1)

        @block.tensor
        def _(pe):
            def spread_sums(t):
                pe.wait_ge(widened, t + 1)
                for f in range(2):
                    if t:
                        pe.wait_ge(scaled, 2 * t - 1 + f)
                    for c in range(4):
                        k = 4 * f + c
                        last = nc.tensor.transpose(ps[:, BB + f, c * P:(c + 1) * P], flat(rb[:, 2 * k:2 * k + 2, :]), ident[:, :])
                    last.then_inc(spread, 1)

            pe.wait_ge(consts, 16 * 5)
            spread_sums(0)
            pe.wait_ge(w_lo, KC)
            for t in range(NB):
                if t + 1 < NB:
                    spread_sums(t + 1)
                pe.wait_ge(m_ready, t + 1)
                if t:
                    pe.wait_ge(gated, t)
                for half in range(2):
                    for k in range(KC):
                        for i, (a, w) in enumerate(((0, 0), (0, 1), (1, 0))):
                            last = nc.tensor.matmul(ps[:, YB + half, :], mT[a][:, k, :], w_out[w][:, k, half * BANK:(half + 1) * BANK],
                                                    start=(k == 0 and i == 0), stop=(k == KC - 1 and i == 2))
                    last.then_inc(y_ready, 1)
                pe.wait_ge(xn_ready, t + 1)
                if t:
                    pe.wait_ge(hv_ready, t)
                for f in range(2):
                    for c in range(4):
                        last = nc.tensor.transpose(ps[:, TB + f, c * P:(c + 1) * P], xn[:, 4 * f + c, :], ident[:, :])
                    last.then_inc(turned, 1)


def mlp_phase(nc, A, scr, h2, out):
    with ExitStack() as ctx:
        sb = lambda n, s, d=F32: ctx.enter_context(nc.sbuf_tensor(n, s, d))
        sem = lambda n: ctx.enter_context(nc.semaphore(n))
        FC = 4
        NCH = NF // FC
        acc = sb("f_acc", [P, NB, D])
        g2 = sb("f_g2", [P, D])
        w1r = sb("f_w1r", [P, KC, P])
        w2r = sb("f_w2r", [P, D])
        w1 = [sb(f"f_w1{i}", [P, 2, KC, P], F32R) for i in range(2)]
        w2 = [sb(f"f_w2{i}", [P, FC, D], F32R) for i in range(2)]
        r = sb("f_r", [P, SEQ])
        a = sb("f_a", [P, SEQ])
        aT = [sb(f"f_aT{i}", [P, FC, SEQ], F32R) for i in range(2)]
        tmp = sb("f_tmp", [P, D])
        ps = ctx.enter_context(nc.psum_tensor("f_ps", [P, 8, BANK], F32))
        consts = sem("f_consts")
        acc_loaded = sem("f_acc_loaded")
        w1_loaded = sem("f_w1_loaded")
        w2_loaded = sem("f_w2_loaded")
        w1_hi = sem("f_w1_hi")
        w1_ready = sem("f_w1_ready")
        w2_hi = sem("f_w2_hi")
        w2_ready = sem("f_w2_ready")
        up_ready = sem("f_up_ready")
        rect = sem("f_rect")
        a_hi = sem("f_a_hi")
        a_square = sem("f_a_square")
        a_ready = sem("f_a_ready")
        down_ready = sem("f_down_ready")
        gated = sem("f_gated")
        added = sem("f_added")
        stored = sem("f_stored")
        block = ctx.enter_context(nc.Block())
        w1_dram = A["w_mlp1"][0].rearrange("(k p) (f c) -> f p k c", p=P, c=P)
        w2_dram = A["w_mlp2"][0].rearrange("(f p) n -> f p n", p=P)

        @block.sync
        def _(sp):
            def load_w1(g, wait=True):
                if wait:
                    sp.wait_ge(w1_ready, g)
                sp.dma_start(w1r[:, :, :], w1_dram[bass.ds(g, 1)].rearrange("f p k c -> p (f k) c")).then_inc(w1_loaded, 16)

            def load_w2(g, wait=True):
                if wait:
                    sp.wait_ge(w2_ready, g)
                sp.dma_start(w2r[:, :], w2_dram[bass.ds(g, 1)].rearrange("f p n -> p (f n)")).then_inc(w2_loaded, 16)

            load_w1(0, wait=False)
            load_w2(0, wait=False)
            sp.dma_start(g2[:, :], scr["mod"][0:1, 5 * D:6 * D].partition_broadcast(P).rearrange("p a n -> p (a n)")).then_inc(consts, 16)
            sp.dma_start(acc[:, :, :], scr["x1"].rearrange("(t p) n -> p t n", p=P)).then_inc(acc_loaded, 16)
            load_w1(1)
            load_w2(1)
            with sp.Fori(2, NF) as g:
                load_w1(g)
                load_w2(g)
            for t in range(NB):
                sp.wait_ge(added, (NCH - 1) * NB + t + 1)
                sp.dma_start(out[0, t * P:(t + 1) * P, :], acc[:, t, :]).then_inc(stored, 16)
            sp.wait_ge(stored, 16 * NB)

        @block.scalar
        def _(act):
            def w1_high(g, slot, wait=True):
                act.wait_ge(w1_loaded, g * 16 + 16)
                if wait:
                    act.wait_ge(up_ready, g - 1)
                nc.scalar.activation(w1[0][:, slot, :, :], w1r[:, :, :], ACT.Copy).then_inc(w1_hi, 1)

            def w2_high(g, f, ch, wait=True):
                act.wait_ge(w2_loaded, g * 16 + 16)
                if wait and f == 0:
                    act.wait_ge(down_ready, ch * NB)
                nc.scalar.activation(w2[0][:, f, :], w2r[:, :], ACT.Copy).then_inc(w2_hi, 1)

            def turn(ch, g0, first, last):
                for f in range(FC):
                    g = g0 + f
                    if not (last and f == FC - 1):
                        w1_high(g + 1, (f + 1) % 2, wait=not (first and f == 0))
                    w2_high(g, f, ch, wait=not first)
                    act.wait_ge(up_ready, g + 1)
                    if not (first and f == 0):
                        act.wait_ge(a_ready, g)
                    b = 2 * (f % 2)
                    nc.scalar.activation(r[:, :], flat(ps[:, b:b + 2, :]), ACT.Relu).then_inc(rect, 1)
                    act.wait_ge(rect, g + 1)
                    nc.scalar.activation(aT[0][:, f, :], r[:, :], ACT.Square).then_inc(a_hi, 1)

            w1_high(0, 0, wait=False)
            turn(0, 0, True, False)
            with act.Fori(1, NCH - 1) as ch:
                turn(ch, ch * FC, False, False)
            turn(NCH - 1, NF - FC, False, True)

        @block.vector
        def _(dve):
            V = nc.vector

            def w1_low(g, slot):
                dve.wait_ge(w1_hi, g + 1)
                V.tensor_tensor(w1[1][:, slot, :, :], w1r[:, :, :], w1[0][:, slot, :, :].bitcast(F32),
                                ALU.subtract).then_inc(w1_ready, 1)

            def turn(ch, g0, first, last):
                for f in range(FC):
                    g = g0 + f
                    if not (last and f == FC - 1):
                        w1_low(g + 1, (f + 1) % 2)
                    dve.wait_ge(w2_hi, g + 1)
                    V.tensor_tensor(w2[1][:, f, :], w2r[:, :], w2[0][:, f, :].bitcast(F32), ALU.subtract).then_inc(w2_ready, 1)
                    dve.wait_ge(rect, g + 1)
                    if not (first and f == 0):
                        dve.wait_ge(a_ready, g)
                    V.tensor_tensor(a[:, :], r[:, :], r[:, :], ALU.mult).then_inc(a_square, 1)
                    dve.wait_ge(a_square, g + 1)
                    dve.wait_ge(a_hi, g + 1)
                    V.tensor_tensor(aT[1][:, f, :], a[:, :], aT[0][:, f, :].bitcast(F32), ALU.subtract).then_inc(a_ready, 1)
                for t in range(NB):
                    n = ch * NB + t
                    dve.wait_ge(down_ready, n + 1)
                    b = 4 + 2 * (t % 2)
                    if not (first and t == 0):
                        dve.wait_ge(added, n)
                    V.tensor_tensor(tmp[:, :], flat(ps[:, b:b + 2, :]), g2[:, :], ALU.mult).then_inc(gated, 1)
                    dve.wait_ge(gated, n + 1)
                    V.tensor_tensor(acc[:, t, :], acc[:, t, :], tmp[:, :], ALU.add).then_inc(added, 1)

            w1_low(0, 0)
            dve.wait_ge(consts, 16)
            dve.wait_ge(acc_loaded, 16)
            turn(0, 0, True, False)
            with dve.Fori(1, NCH - 1) as ch:
                turn(ch, ch * FC, False, False)
            turn(NCH - 1, NF - FC, False, True)

        @block.tensor
        def _(pe):
            def up(g, f, wait):
                slot, b = f % 2, 2 * (f % 2)
                pe.wait_ge(w1_ready, g + 1)
                if wait:
                    pe.wait_ge(rect, g - 1)
                for k in range(KC):
                    for i, (x, w) in enumerate(((0, 0), (1, 0), (0, 1))):
                        for half in range(2):
                            last = nc.tensor.matmul(ps[:, b + half, :], w1[w][:, slot, k, :],
                                                    h2[x][:, k, half * BANK:(half + 1) * BANK],
                                                    start=(k == 0 and i == 0), stop=(k == KC - 1 and i == 2))
                last.then_inc(up_ready, 1)

            def down(n, t, g0, wait):
                b = 4 + 2 * (t % 2)
                if wait:
                    pe.wait_ge(gated, n - 1)
                for f in range(FC):
                    if t == 0:
                        pe.wait_ge(a_ready, g0 + f + 1)
                        pe.wait_ge(w2_ready, g0 + f + 1)
                    for i, (x, w) in enumerate(((0, 0), (0, 1), (1, 0))):
                        for half in range(2):
                            last = nc.tensor.matmul(ps[:, b + half, :], aT[x][:, f, t * P:(t + 1) * P],
                                                    w2[w][:, f, half * BANK:(half + 1) * BANK],
                                                    start=(f == 0 and i == 0), stop=(f == FC - 1 and i == 2))
                last.then_inc(down_ready, 1)

            def turn(ch, g0, first):
                for f in range(FC):
                    up(g0 + f, f, not (first and f < 2))
                for t in range(NB):
                    down(ch * NB + t, t, g0, not (first and t < 2))

            turn(0, 0, True)
            with pe.Fori(1, NCH) as ch:
                turn(ch, ch * FC, False)


def layer(nc, A, out):
    scratch = lambda n, s: nc.dram_tensor(f"scratch_{n}", s, F32, kind="Internal").ap()
    scr = {
        "mod": scratch("mod", (2, 6 * D)),
        "q": scratch("q", (HEADS, QK, 2, KALL)),
        "k": scratch("k", (HEADS, QK, 2, KALL)),
        "v": scratch("v", (HEADS, NT, P, 2 * VD)),
        "sq": scratch("sq", (NT, P, SH * P)),
        "sk": scratch("sk", (SKV, 2, P, CTX + SEQ + 2 * P)),
        "sv": scratch("sv", (NT + 2, P, SKV * P)),
        "x1": scratch("x1", (SEQ, D)),
    }
    modulation_phase(nc, A, scr)
    token_phase(nc, A, scr)
    with ExitStack() as ctx:
        h2 = [ctx.enter_context(nc.sbuf_tensor(f"h2_{i}", [P, KC, SEQ], F32R)) for i in range(2)]
        with ExitStack() as inner:
            mix = inner.enter_context(nc.sbuf_tensor("mix", [P, KC, SEQ], F32))
            rs = inner.enter_context(nc.sbuf_tensor("rs", [P, NB, HEADS + SH], F32))
            swa_phase(nc, A, scr, mix, rs)
            mla_phase(nc, A, scr, mix, rs)
            out_phase(nc, A, scr, mix, rs, h2)
        mlp_phase(nc, A, scr, h2, out)


INS = ["x", "c", "ctx", "c_ctx", "w_mod", "b_mod", "g_attn", "w_in", "g_q_a", "w_uq", "g_kv_a", "w_ukv", "g_mla_q",
       "g_mla_k", "g_swa_q", "g_swa_k", "swa_sink", "w_out", "g_mlp", "w_mlp1", "w_mlp2"]


def shape_constants():
    import numpy as np
    grid = 64

    def rope(dim):
        n = dim // 4
        inv = (np.float32(10000.0) ** (-np.arange(n, dtype=np.float32) / np.float32(n))).astype(np.float32)
        tok = np.arange(SEQ)
        row, col = (tok // grid).astype(np.float32), (tok % grid).astype(np.float32)
        ang = np.concatenate([row[:, None] * inv, col[:, None] * inv], axis=1).astype(np.float32).astype(np.float64)
        cos, sin = np.cos(ang), np.sin(ang)
        cos = np.concatenate([np.ones((CTX, dim // 2)), cos]).astype(np.float32)
        sin = np.concatenate([np.zeros((CTX, dim // 2)), sin]).astype(np.float32)
        return np.concatenate([cos, cos, -sin, sin], axis=1)

    table = np.concatenate([rope(ROPE), rope(SD)], axis=1).astype(np.float32)
    q = np.arange(P)[None, :, None] + P * np.arange(NB)[:, None, None]
    k = np.arange(3 * P)[None, None, :] - P + P * np.arange(NB)[:, None, None]
    valid = (np.abs(q - k) <= P) & (k >= 0) & (k < SEQ)
    return {"ident": np.eye(P, dtype=np.float32), "rope": table,
            "mask": np.where(valid, np.float32(0), np.float32(-1e30)).astype(np.float32)}


def kernel(**inputs):
    import numpy as np
    import concourse.bacc as bacc
    from concourse.bass_utils import run_bass_kernel_spmd

    nc = bacc.Bacc("TRN2", target_bir_lowering=False, num_devices=1)
    host = {n: np.ascontiguousarray(inputs[n]) for n in INS}
    host.update(shape_constants())
    arrays = {f"in_{n}": v for n, v in host.items()}
    A = {n: nc.dram_tensor(f"in_{n}", v.shape, mybir.dt.from_np(v.dtype), kind="ExternalInput").ap() for n, v in host.items()}
    out = nc.dram_tensor("out_0", (1, SEQ, D), F32, kind="ExternalOutput").ap()
    layer(nc, A, out)
    r = run_bass_kernel_spmd(nc, [arrays], core_ids=[0])
    return r.results[0]["out_0"]
```

```python
from contextlib import ExitStack

import concourse.bass as bass
from concourse import mybir

F32 = mybir.dt.float32
F32R = mybir.dt.float32r
ALU = mybir.AluOpType
ACT = mybir.ActivationFunctionType
AX = mybir.AxisListType

P = 128
BANK = 512
D = 1024
KC = D // P
SEQ = 1024
CTX = 256
NT = (SEQ + CTX) // P
NCT = CTX // P
NB = SEQ // P
HEADS = 8
NOPE, ROPE, QK, VD = 64, 32, 96, 64
QL, KVL = 256, 128
SH, SKV, SD = 8, 2, 64
IN_W = QL + KVL + ROPE + SH * SD + 2 * SKV * SD
FF = 4096
NF = FF // P
KALL = SEQ + CTX
EPS = 1e-6
MLA_SCALE = QK ** -0.5
SWA_SCALE = SD ** -0.5
NS = SH + SKV
ZCH = ((0, 416), (416, 928), (928, 1184))
SPILLS = 7
UNITK = 5
GRP = SH // SKV


class Chain:

    def __init__(self, eng, sem):
        self.eng, self.sem, self.n, self.base = eng, sem, 0, 0

    def __call__(self, ins):
        self.n += 1
        ins.then_inc(self.sem, 1)
        self.eng.wait_ge(self.sem, self.base + self.n)

    def mark(self, ins):
        self.n += 1
        ins.then_inc(self.sem, 1)

    def reach(self):
        self.eng.wait_ge(self.sem, self.base + self.n)

    def enter(self, turn, per):
        self.start, self.per = self.base + self.n, per
        self.base, self.n = self.start + turn * per, 0

    def leave(self, turns):
        assert self.n == self.per, ("instructions per turn", self.n)
        self.base, self.n = self.start + turns * self.per, 0


def bc(ap, n):
    return ap.unsqueeze(len(ap.shape)).to_broadcast(tuple(ap.shape) + (n,))


def mid(ap, n):
    return ap.unsqueeze(1).to_broadcast((ap.shape[0], n, ap.shape[1]))


def flat(ap):
    return ap.rearrange("p a b -> p (a b)")


def modulation_phase(nc, A, scr, w_in, w_uq, w_kv):
    NW = 6 * D
    WR = 3
    with ExitStack() as ctx:
        sb = lambda n, s, d=F32: ctx.enter_context(nc.sbuf_tensor(n, s, d))
        sem = lambda n: ctx.enter_context(nc.semaphore(n))
        wm = sb("m_w", [P, WR, NW])
        cc = sb("m_c", [P, KC, 2])
        ex = sb("m_e", [P, KC, 2])
        sT = sb("m_s", [P, KC, 32])
        bm = sb("m_b", [P, 3, BANK])
        mo = sb("m_o", [P, 3, BANK])
        ps = ctx.enter_context(nc.psum_tensor("m_ps", [P, 3, BANK], F32))
        c_loaded = sem("m_c_loaded")
        b_loaded = sem("m_b_loaded")
        w_loaded = [sem(f"m_w_loaded{i}") for i in range(WR)]
        cleared = sem("m_cleared")
        exped = sem("m_exped")
        silu_ready = sem("m_silu_ready")
        chain = sem("m_chain")
        w_used = sem("m_w_used")
        summed = sem("m_summed")
        stored = sem("m_stored")
        PR = 3
        raw = sb("m_raw", [P, PR, IN_W])
        p_loaded = [sem(f"m_p_loaded{i}") for i in range(PR)]
        hi_done = sem("m_hi_done")
        lo_done = sem("m_lo_done")
        jobs = [(A["w_in"][0, k * P:(k + 1) * P, :], w_in[0][:, k, :], w_in[1][:, k, :], IN_W) for k in range(KC)]
        jobs += [(A["w_uq"][0, k * P:(k + 1) * P, :], w_uq[0][:, k, :], w_uq[1][:, k, :], HEADS * QK) for k in range(2)]
        jobs += [(A["w_ukv"][0], w_kv[0][:, :], w_kv[1][:, :], HEADS * P)]
        block = ctx.enter_context(nc.Block())

        @block.sync
        def _(sp):
            with nc.allow_non_contiguous_dma(reason="two small vectors"):
                sp.dma_start(cc[:, :, 0], A["c"].rearrange("b (k p) -> p (b k)", p=P)).then_inc(c_loaded, 16)
                sp.dma_start(cc[:, :, 1], A["c_ctx"].rearrange("(k p) -> p k", p=P)).then_inc(c_loaded, 16)
            for k in range(KC):
                if k >= WR:
                    sp.wait_ge(w_used, k - WR + 1)
                sp.dma_start(wm[:, k % WR, :], A["w_mod"][0, k * P:(k + 1) * P, :]).then_inc(w_loaded[k % WR], 16)
                for i in range(k * len(jobs) // KC, (k + 1) * len(jobs) // KC):
                    if i >= PR:
                        sp.wait_ge(lo_done, i - PR + 1)
                    sp.dma_start(raw[:, i % PR, 0:jobs[i][3]], jobs[i][0]).then_inc(p_loaded[i % PR], 16)
            sp.wait_ge(summed, 1)
            for j in range(4):
                sp.dma_start(scr["mod"].rearrange("r (b j n) -> j r b n", b=3, j=4)[j],
                             mo[32 * j:32 * j + 2, :, :]).then_inc(stored, 16)
            sp.wait_ge(stored, 64)

        @block.gpsimd
        def _(pool):
            nc.gpsimd.memset(flat(sT[:, :, :]), 0.0).then_inc(cleared, 1)
            nc.gpsimd.memset(flat(bm[:, :, :]), 0.0).then_inc(cleared, 1)
            pool.wait_ge(cleared, 2)
            for j in range(4):
                for r in range(2):
                    pool.dma_start(bm[32 * j + r:32 * j + r + 1, :, :],
                                   A["b_mod"].rearrange("l (b j n) -> j l b n", b=3, j=4)[j]).then_inc(b_loaded, 16)

        @block.scalar
        def _(act):
            act.wait_ge(c_loaded, 32)
            nc.scalar.activation(flat(ex[:, :, :]), flat(cc[:, :, :]), ACT.Exp, scale=-1.0).then_inc(exped, 1)
            for i, (_, hi, _, n) in enumerate(jobs):
                act.wait_ge(p_loaded[i % PR], 16 * (i // PR + 1))
                nc.scalar.activation(hi, raw[:, i % PR, 0:n], ACT.Copy).then_inc(hi_done, 1)

        @block.vector
        def _(dve):
            link = Chain(dve, chain)
            dve.wait_ge(exped, 1)
            link(nc.vector.tensor_scalar_add(flat(ex[:, :, :]), flat(ex[:, :, :]), 1.0))
            link(nc.vector.reciprocal(flat(ex[:, :, :]), flat(ex[:, :, :])))
            dve.wait_ge(cleared, 1)
            nc.vector.tensor_tensor(sT[:, :, 0:2], cc[:, :, :], ex[:, :, :], ALU.mult).then_inc(silu_ready, 1)
            for i, (_, hi, lo, n) in enumerate(jobs):
                dve.wait_ge(hi_done, i + 1)
                nc.vector.tensor_tensor(lo, raw[:, i % PR, 0:n], hi.bitcast(F32), ALU.subtract).then_inc(lo_done, 1)
            dve.wait_ge(w_used, KC)
            dve.wait_ge(b_loaded, 128)
            nc.vector.tensor_tensor(flat(mo[:, :, :]), flat(ps[:, :, :]), flat(bm[:, :, :]), ALU.add).then_inc(summed, 1)

        @block.tensor
        def _(pe):
            pe.wait_ge(silu_ready, 1)
            for k in range(KC):
                pe.wait_ge(w_loaded[k % WR], 16 * (k // WR + 1))
                for n in range(12):
                    j = n % 4
                    last = nc.tensor.matmul(ps[32 * j:32 * j + 32, n // 4, :], sT[:, k, :],
                                            wm[:, k % WR, n * BANK:(n + 1) * BANK], start=(k == 0), stop=(k == KC - 1))
                last.then_inc(w_used, 1)


def token_phase(nc, A, scr):
    with ExitStack() as ctx:
        sb = lambda n, s, d=F32: ctx.enter_context(nc.sbuf_tensor(n, s, d))
        sem = lambda n: ctx.enter_context(nc.semaphore(n))
        w_in = [sb(f"w_in{i}", [P, KC, IN_W], F32R) for i in range(2)]
        w_uq = [sb(f"w_uq{i}", [P, 2, HEADS * QK], F32R) for i in range(2)]
        w_kv = [sb(f"w_kv{i}", [P, HEADS * P], F32R) for i in range(2)]

        modulation_phase(nc, A, scr, w_in, w_uq, w_kv)
        ident = sb("t_ident", [P, P])
        xt = sb("t_x", [P, 2, D])
        tab = sb("t_rope", [P, 2, 2 * (ROPE + SD)])
        xn = sb("t_xn", [P, KC, P])
        junk = sb("t_junk", [P, D])
        hT = [sb(f"t_h{i}", [P, KC, P], F32R) for i in range(2)]
        zs2 = sb("t_z", [P, 2, IN_W])
        qm = sb("t_q", [P, HEADS, QK])
        kv = sb("t_kv", [P, HEADS, P])
        sqq = sb("t_sqq", [P, HEADS, QK])
        sqk = sb("t_sqk", [P, HEADS, NOPE])
        sqs = sb("t_sqs", [P, NS, SD])
        gq = sb("t_gq", [P, HEADS, QK])
        gk = sb("t_gk", [P, HEADS, NOPE])
        gs = sb("t_gs", [P, NS, SD])
        gr = sb("t_gr", [P, 1, ROPE])
        swq = sb("t_swq", [P, HEADS, ROPE])
        sws = sb("t_sws", [P, NS, SD])
        swr = sb("t_swr", [P, 1, ROPE])
        roq = sb("t_roq", [P, HEADS, ROPE])
        ros = sb("t_ros", [P, NS, SD])
        ror = sb("t_ror", [P, 1, ROPE])
        qn = sb("t_qn", [P, HEADS, QK])
        kn = sb("t_kn", [P, HEADS, QK])
        sn = sb("t_sn", [P, SH + 2 * SKV, SD])
        cn = sb("t_cn", [P, 3, P])
        cT = [sb(f"t_c{i}", [P, 3, P], F32R) for i in range(2)]
        qT = sb("t_qT", [QK, 2, HEADS, P], F32R)
        kT = sb("t_kT", [QK, 2, HEADS, P], F32R)
        sT = sb("t_sT", [P, SH, P], F32R)
        sK = sb("t_sK", [P, 2, SKV, P], F32R)
        vm = sb("t_vm", [P, HEADS, 2 * VD], F32R)
        vs = sb("t_vs", [P, SKV, 2 * SD], F32R)
        stx = sb("t_stx", [P, 1])
        stc = sb("t_stc", [P, 2])
        stn = sb("t_stn", [P, 27])
        mcol = sb("t_mcol", [P, 2, 2, KC])
        gcol = sb("t_gcol", [P, KC])
        b_qa = sb("t_bqa", [P, QL])
        b_kva = sb("t_bkva", [P, KVL])
        b_mq = sb("t_bmq", [P, QK])
        b_mk = sb("t_bmk", [P, QK])
        b_sq = sb("t_bsq", [P, SD])
        b_sk = sb("t_bsk", [P, SD])
        zero = sb("t_zero", [P, 2, SKV, P])
        ps = ctx.enter_context(nc.psum_tensor("t_ps", [P, 8, BANK], F32))
        TB, UB = 3, 5

        consts = sem("t_consts")
        gains = sem("t_gains")
        zeroed = sem("t_zeroed")
        x_loaded = [sem(f"t_x_loaded{i}") for i in range(2)]
        tab_loaded = [sem(f"t_tab_loaded{i}") for i in range(2)]
        squared = sem("t_squared")
        var_ready = sem("t_var_ready")
        root_ready = sem("t_root_ready")
        xn_ready = sem("t_xn_ready")
        filled = sem("t_filled")
        emptied = sem("t_emptied")
        hi_ready = sem("t_hi_ready")
        hv_ready = sem("t_hv_ready")
        h_hi = sem("t_h_hi")
        h_ready = sem("t_h_ready")
        z_ready = sem("t_z_ready")
        z_copied = sem("t_z_copied")
        c_ready = sem("t_c_ready")
        u_ready = sem("t_u_ready")
        u_copied = sem("t_u_copied")
        gained = sem("t_gained")
        normed = sem("t_normed")
        v_hi = sem("t_v_hi")
        spilled = sem("t_spilled")
        v_spilled = sem("t_v_spilled")
        pads = sem("t_pads")
        v_chain = sem("t_v_chain")
        g_chain = sem("t_g_chain")
        def FILL(t, k):
            if isinstance(t, int) and t == 0:
                return 2 + k
            if isinstance(t, int) and t == NT:
                return 10 * t - 10 + k
            if isinstance(t, int) and t == NT - 1 and k > 2:
                return 10 * t - 7 + k
            return t * 10 + (k - 5)

        def side(t, k):
            return k % 2 if isinstance(t, int) and t in (0, NT) else (k + 1) % 2

        def HI(t, k):
            if isinstance(t, int) and t == 0:
                return 0
            if isinstance(t, int) and t == NT:
                return 8 * t - 10 + k
            return t * 8 + (-7 if k == 0 else k - 9)

        def EV(t, k):
            if isinstance(t, int) and t == NT - 1:
                return 3 * t + 2
            if isinstance(t, int) and t == NT - 2 and k == 2:
                return 3 * t + 4
            return t * 3 + (3 + k)

        block = ctx.enter_context(nc.Block())

        @block.sync
        def _(sp):
            def load_x(t, b):
                src = A["ctx"][0, t * P:(t + 1) * P, :] if isinstance(t, int) and t < NCT else \
                    A["x"][0, bass.ds((t - NCT) * P, P), :]
                sp.dma_start(xt[:, b, :], src).then_inc(x_loaded[b], 16)

            def load_tab(t, b):
                sp.dma_start(tab[:, b, :], A["rope"][bass.ds(t * P, P), :]).then_inc(tab_loaded[b], 16)

            def step(t, b, load=True):
                if load and not (isinstance(t, int) and t > NT - 3):
                    sp.wait_ge(xn_ready, t + 1)
                    load_x(t + 2, b)
                if load:
                    if not (isinstance(t, int) and t == 0):
                        sp.wait_ge(normed, t)
                    load_tab(t + 1, 1 - b)
                if isinstance(t, int) and t == 0:
                    return
                u = t - 1
                sp.wait_ge(normed, t)
                sp.dma_start(scr["v"][:, bass.ds(u, 1), :, :].rearrange("h a p c -> p (h a) c"),
                             vm[:, :, :].bitcast(F32)).then_inc(v_spilled, 16)
                vt = u if isinstance(u, int) and u < NCT else u + 1
                sp.dma_start(scr["sv"][bass.ds(vt, 1)].rearrange("a p c -> p (a c)"),
                             flat(vs[:, :, :]).bitcast(F32)).then_inc(v_spilled, 16)
                sp.wait_ge(emptied, FILL(t, 9) + 1)
                cols = bass.ds(u * P, P)
                for i in range(2):
                    sp.dma_start(scr["q"][:, :, i, cols].rearrange("h p c -> p h c"),
                                 qT[:, i, :, :].bitcast(F32)).then_inc(spilled, 16)
                    sp.dma_start(scr["k"][:, :, i, cols].rearrange("h p c -> p h c"),
                                 kT[:, i, :, :].bitcast(F32)).then_inc(spilled, 16)
                    kcols = bass.ds(u * P + (0 if isinstance(u, int) and u < NCT else P), P)
                    sp.dma_start(scr["sk"][:, i, :, kcols].rearrange("v p c -> p v c"),
                                 sK[:, i, :, :].bitcast(F32)).then_inc(spilled, 16)
                sp.dma_start(scr["sq"][bass.ds(u, 1)].rearrange("a p c -> p (a c)"),
                             sT[:, :, :].rearrange("p h c -> p (h c)").bitcast(F32)).then_inc(spilled, 16)

            load_x(0, 0)
            sp.dma_start(ident[:, :], A["ident"]).then_inc(consts, 16)
            with nc.allow_non_contiguous_dma(reason="a few vectors, one element a row"):
                for s in range(2):
                    for r in range(2):
                        sp.dma_start(mcol[:, s, r, :],
                                     scr["mod"][r, s * D:(s + 1) * D].rearrange("(k p) -> p k", p=P)).then_inc(consts, 16)
                sp.dma_start(gcol[:, :], A["g_attn"].rearrange("l (k p) -> p (l k)", p=P)).then_inc(consts, 16)
            load_x(1, 1)
            load_tab(0, 0)
            for dst, name in ((b_qa, "g_q_a"), (b_kva, "g_kv_a"), (b_mq, "g_mla_q"), (b_mk, "g_mla_k"),
                              (b_sq, "g_swa_q"), (b_sk, "g_swa_k")):
                sp.dma_start(dst[:, :], A[name].partition_broadcast(P).rearrange("p a n -> p (a n)")).then_inc(gains, 16)
            for t in range(NT + 1):
                step(t, t % 2, load=t < NT - 1)
            sp.wait_ge(zeroed, 1)
            for e in (CTX, CTX + P + SEQ):
                sp.dma_start(scr["sk"][:, :, :, e:e + P].rearrange("v i p c -> p (v i) c"),
                             zero[:, :, :, :].rearrange("p i v c -> p (i v) c")).then_inc(pads, 16)
            for e in (NCT, NT + 1):
                sp.dma_start(scr["sv"][e], zero[:, :, :, :].rearrange("p i v c -> p (i v c)")[:, 0:SKV * P]).then_inc(pads, 16)
            sp.wait_ge(pads, 64)
            sp.wait_ge(spilled, 16 * SPILLS * NT)
            sp.wait_ge(v_spilled, 32 * NT)

        @block.gpsimd
        def _(pool):
            link = Chain(pool, g_chain)
            nc.gpsimd.memset(zero[:, :, :, :].rearrange("p i v c -> p (i v c)"), 0.0).then_inc(zeroed, 1)
            pool.wait_ge(gains, 16 * 6)

            def swap(out, x, sin, n, h):
                nc.gpsimd.tensor_tensor(out[:, :, 0:h], x[:, :, h:2 * h], mid(sin[:, 0:h], n), ALU.mult)
                return nc.gpsimd.tensor_tensor(out[:, :, h:2 * h], x[:, :, 0:h], mid(sin[:, h:2 * h], n), ALU.mult)

            def step(t, b, turn):
                zs = zs2[:, b, :]
                pool.wait_ge(z_copied, t * 3 + 3)
                if not (isinstance(t, int) and t == 0):
                    pool.wait_ge(normed, t)
                nc.gpsimd.tensor_tensor(gs[:, 0:SH, :], zs[:, 416:928].rearrange("p (h d) -> p h d", h=SH),
                                        mid(b_sq[:, :], SH), ALU.mult)
                nc.gpsimd.tensor_tensor(gs[:, SH:NS, :], zs[:, 928:1056].rearrange("p (h d) -> p h d", h=SKV),
                                        mid(b_sk[:, :], SKV), ALU.mult)
                link(nc.gpsimd.tensor_tensor(gr[:, 0, :], zs[:, 384:416], b_mk[:, NOPE:QK], ALU.mult))
                pool.wait_ge(tab_loaded[b], turn * 16 + 16)
                tb = tab[:, b, :]
                swap(swr, gr, tb[:, ROPE:2 * ROPE], 1, ROPE // 2)
                swap(sws, gs, tb[:, 2 * ROPE + SD:], NS, SD // 2)
                pool.wait_ge(u_copied, t * 4 + 4)
                link(nc.gpsimd.tensor_tensor(gq[:, :, :], qm[:, :, :], mid(b_mq[:, :], HEADS), ALU.mult))
                nc.gpsimd.tensor_tensor(gk[:, :, :], kv[:, :, 0:NOPE], mid(b_mk[:, 0:NOPE], HEADS), ALU.mult)
                swap(swq, gq[:, :, NOPE:QK], tb[:, ROPE:2 * ROPE], HEADS, ROPE // 2).then_inc(gained, 1)

            for t in range(2):
                step(t, t, 0)
            with pool.Fori(1, NT // 2) as i:
                link.enter(i - 1, 4)
                step(i * 2, 0, i)
                step(i * 2 + 1, 1, i)
                link.leave(NT // 2 - 1)

        @block.scalar
        def _(act):
            def root(e, st):
                act.wait_ge(var_ready, e + 1)
                nc.scalar.activation(st, st, ACT.Sqrt).then_inc(root_ready, 1)

            def square_x(b, turn):
                act.wait_ge(x_loaded[b], turn * 16 + 16)
                nc.scalar.activation(junk[:, :], xt[:, b, :], ACT.Square, accum_out=stx[:, :]).then_inc(squared, 1)

            def hi_fills(t):
                for k in range(3, 10):
                    src = ps[:, TB + side(t, k), :]
                    act.wait_ge(filled, FILL(t, k) + 1)
                    if k == 3 and not (isinstance(t, int) and t == 1):
                        act.wait_ge(spilled, (t - 1) * 16 * SPILLS)
                    if k < 7:
                        h0 = 4 * ((k - 3) % 2)
                        o = (qT, kT)[(k - 3) // 2][:, 0, h0:h0 + 4, :]
                        ins = nc.scalar.activation(o.rearrange("p h c -> p (h c)"), src[0:QK, :], ACT.Copy)
                    elif k < 9:
                        for r in range(2):
                            ins = nc.scalar.activation(sT[0:SD, 4 * (k - 7):4 * (k - 7) + 4, :].rearrange("p (g r) c -> p r g c", r=2)[:, r],
                                                       src[SD * r:SD * r + SD, 0:2 * P].rearrange("p (g c) -> p g c", g=2), ACT.Copy)
                    else:
                        ins = nc.scalar.activation(flat(sK[:, 0, :, :]), src[:, 0:SKV * P], ACT.Copy)
                    ins.then_inc(hi_ready, 1)

            def high_x(t):
                act.wait_ge(hv_ready, t + 1)
                nc.scalar.activation(flat(hT[0][:, :, :]), flat(xn[:, :, :]), ACT.Copy).then_inc(h_hi, 1)

            def take_z(t, b, e):
                zs = zs2[:, b, :]

                def copy(j):
                    lo, hi = ZCH[j]
                    act.wait_ge(z_ready, t * 3 + j + 1)
                    nc.scalar.activation(zs[:, lo:hi], ps[:, j, 0:hi - lo], ACT.Copy).then_inc(z_copied, 1)

                if not (isinstance(t, int) and t < 2):
                    act.wait_ge(normed, t - 1)
                copy(0)
                copy(1)
                act.wait_ge(z_copied, t * 3 + 2)
                nc.scalar.activation(junk[:, 384:416], zs[:, 384:416], ACT.Square, accum_out=stn[:, 26:27])
                nc.scalar.activation(junk[:, 0:QL], zs[:, 0:QL], ACT.Square, accum_out=stc[:, 0:1])
                nc.scalar.activation(junk[:, QL:384], zs[:, QL:384], ACT.Square, accum_out=stc[:, 1:2]).then_inc(squared, 1)
                root(e, stc[:, :])
                copy(2)
                act.wait_ge(z_copied, t * 3 + 3)
                nc.scalar.activation(sqs[:, :, :].rearrange("p h d -> p (h d)"), zs[:, 416:1056], ACT.Square)

            def step(t, b, xturn):
                first = isinstance(t, int) and t == 0
                last = isinstance(t, int) and t == NT - 1
                zs = zs2[:, b, :]
                act.wait_ge(filled, FILL(t, 0) + 1)
                nc.scalar.activation(flat(cT[0][:, :, :]), ps[:, TB + side(t, 0), 0:3 * P], ACT.Copy).then_inc(hi_ready, 1)
                if not last:
                    high_x(t + 1)
                if not first:
                    act.wait_ge(normed, t)
                for j in range(4):
                    act.wait_ge(u_ready, t * 4 + j + 1)
                    if j < 2:
                        nc.scalar.activation(flat(qm[:, 4 * j:4 * j + 4, :]), ps[:, UB + j, 0:4 * QK],
                                             ACT.Copy).then_inc(u_copied, 1)
                    else:
                        nc.scalar.activation(flat(kv[:, 4 * j - 8:4 * j - 4, :]), ps[:, UB + j % 3 if j < 3 else UB, :],
                                             ACT.Copy).then_inc(u_copied, 1)
                act.wait_ge(u_copied, t * 4 + 4)
                nc.scalar.activation(flat(sqq[:, :, :]), flat(qm[:, :, :]), ACT.Square)
                nc.scalar.activation(sqk[:, :, :], kv[:, :, 0:NOPE], ACT.Square).then_inc(squared, 1)
                if xturn is not None:
                    square_x(b, xturn)
                if not first:
                    act.wait_ge(v_spilled, t * 32)
                nc.scalar.activation(vm[:, :, 0:VD], kv[:, :, NOPE:P], ACT.Copy)
                nc.scalar.activation(vs[:, :, 0:SD], zs[:, 1056:1184].rearrange("p (v d) -> p v d", v=SKV),
                                     ACT.Copy).then_inc(v_hi, 1)
                root(EV(t, 0), stn[:, 0:26])
                if xturn is not None:
                    root(EV(t, 1), stx[:, :])
                if not first:
                    hi_fills(t)
                if not last:
                    take_z(t + 1, 1 - b, EV(t, 2))

            square_x(0, 0)
            root(0, stx[:, :])
            high_x(0)
            square_x(1, 0)
            root(1, stx[:, :])
            take_z(0, 0, 2)
            step(0, 0, 1)
            step(1, 1, 1)
            with act.Fori(1, NT // 2 - 1) as i:
                step(i * 2, 0, i + 1)
                step(i * 2 + 1, 1, i + 1)
            step(NT - 2, 0, None)
            step(NT - 1, 1, None)
            hi_fills(NT)

        @block.vector
        def _(dve):
            V = nc.vector
            link = Chain(dve, v_chain)

            def x_norm(e, t, b):
                dve.wait_ge(squared, e + 1)
                V.tensor_scalar(stx[:, :], stx[:, :], 1.0 / D, EPS, ALU.mult, ALU.add).then_inc(var_ready, 1)
                dve.wait_ge(root_ready, e + 1)
                link(V.reciprocal(stx[:, :], stx[:, :]))
                if not (isinstance(t, int) and t == 0):
                    dve.wait_ge(h_ready, t)
                V.tensor_scalar(flat(xn[:, :, :]), xt[:, b, :], stx[:, 0:1], None, ALU.mult).then_inc(xn_ready, 1)

            def modulate(t, fill0, cond, banks):
                for f in range(2):
                    ks = slice(4 * f, 4 * f + 4)
                    dve.wait_ge(filled, fill0 + f + 1)
                    V.tensor_tensor(xn[:, ks, :], ps[:, TB + banks[f], :].rearrange("p (k c) -> p k c", k=4),
                                    bc(mcol[:, 1, cond, ks], P), ALU.mult).then_inc(emptied, 1)
                dve.wait_ge(emptied, fill0 + 2)
                V.tensor_tensor(xn[:, :, :], xn[:, :, :], bc(mcol[:, 0, cond, :], P), ALU.add).then_inc(hv_ready, 1)
                dve.wait_ge(h_hi, t + 1)
                V.tensor_tensor(flat(hT[1][:, :, :]), flat(xn[:, :, :]), flat(hT[0][:, :, :]).bitcast(F32),
                                ALU.subtract).then_inc(h_ready, 1)

            def lo_fills(t):
                for k in range(3, 10):
                    src = ps[:, TB + side(t, k), :]
                    dve.wait_ge(hi_ready, HI(t, k) + 1)
                    if k < 7:
                        x = (qT, kT)[(k - 3) // 2]
                        hs = slice(4 * ((k - 3) % 2), 4 * ((k - 3) % 2) + 4)
                        ins = V.tensor_tensor(x[:, 1, hs, :].rearrange("p h c -> p (h c)"), src[0:QK, :],
                                              x[:, 0, hs, :].rearrange("p h c -> p (h c)").bitcast(F32), ALU.subtract)
                    elif k < 9:
                        hs = slice(4 * (k - 7), 4 * (k - 7) + 4)
                        for r in range(2):
                            hi, lo = (sT[SD * i:SD * i + SD, hs, :].rearrange("p (g r) c -> p r g c", r=2)[:, r] for i in range(2))
                            ins = V.tensor_tensor(lo, src[SD * r:SD * r + SD, 0:2 * P].rearrange("p (g c) -> p g c", g=2),
                                                  hi.bitcast(F32), ALU.subtract)
                    else:
                        ins = V.tensor_tensor(flat(sK[:, 1, :, :]), src[:, 0:SKV * P], flat(sK[:, 0, :, :]).bitcast(F32),
                                              ALU.subtract)
                    ins.then_inc(emptied, 1)

            def c_norm(e, b):
                zs = zs2[:, b, :]
                dve.wait_ge(squared, e + 1)
                V.tensor_scalar(stc[:, 0:1], stc[:, 0:1], 1.0 / QL, EPS, ALU.mult, ALU.add)
                V.tensor_scalar(stc[:, 1:2], stc[:, 1:2], 1.0 / KVL, EPS, ALU.mult, ALU.add).then_inc(var_ready, 1)
                dve.wait_ge(root_ready, e + 1)
                link(V.reciprocal(stc[:, :], stc[:, :]))
                V.scalar_tensor_tensor(out=flat(cn[:, 0:2, :]), in0=zs[:, 0:QL], scalar=stc[:, 0:1], in1=b_qa[:, :],
                                       op0=ALU.mult, op1=ALU.mult).then_inc(c_ready, 1)
                V.scalar_tensor_tensor(out=cn[:, 2, :], in0=zs[:, QL:384], scalar=stc[:, 1:2], in1=b_kva[:, :],
                                       op0=ALU.mult, op1=ALU.mult).then_inc(c_ready, 1)

            def step(t, b):
                first = isinstance(t, int) and t == 0
                last = isinstance(t, int) and t == NT - 1
                zs = zs2[:, b, :]
                dve.wait_ge(hi_ready, HI(t, 0) + 1)
                V.tensor_tensor(flat(cT[1][:, :, :]), ps[:, TB + side(t, 0), 0:3 * P], flat(cT[0][:, :, :]).bitcast(F32),
                                ALU.subtract).then_inc(emptied, 1)
                if not last:
                    modulate(t + 1, FILL(t, 1), 1 if first else 0, [side(t, 1), side(t, 2)])
                dve.wait_ge(squared, EV(t, 0) + 1)
                V.tensor_reduce(stn[:, 16:26], sqs[:, :, :], AX.X, ALU.add)
                V.tensor_reduce(stn[:, 0:8], sqq[:, :, :], AX.X, ALU.add)
                link(V.tensor_reduce(stn[:, 8:16], sqk[:, :, :], AX.X, ALU.add))
                link(V.tensor_scalar(stn[:, 8:16], stn[:, 8:16], stn[:, 26:27], None, ALU.add))
                V.tensor_scalar(stn[:, 0:16], stn[:, 0:16], 1.0 / QK, EPS, ALU.mult, ALU.add)
                V.tensor_scalar(stn[:, 16:26], stn[:, 16:26], 1.0 / SD, EPS, ALU.mult, ALU.add).then_inc(var_ready, 1)
                if not (isinstance(t, int) and t >= NT - 2):
                    x_norm(EV(t, 1), t + 2, b)
                if not first:
                    lo_fills(t)
                dve.wait_ge(v_hi, t + 1)
                V.tensor_tensor(vm[:, :, VD:2 * VD], kv[:, :, NOPE:P], vm[:, :, 0:VD].bitcast(F32), ALU.subtract)
                V.tensor_tensor(vs[:, :, SD:2 * SD], zs[:, 1056:1184].rearrange("p (v d) -> p v d", v=SKV),
                                vs[:, :, 0:SD].bitcast(F32), ALU.subtract)
                dve.wait_ge(root_ready, EV(t, 0) + 1)
                link(V.reciprocal(stn[:, 0:26], stn[:, 0:26]))
                link(V.tensor_scalar(stn[:, 0:8], stn[:, 0:8], MLA_SCALE, None, ALU.mult))
                link(V.tensor_scalar(stn[:, 16:24], stn[:, 16:24], SWA_SCALE, None, ALU.mult))
                dve.wait_ge(gained, t + 1)
                tb = tab[:, b, :]
                V.tensor_tensor(ror[:, :, :], gr[:, :, :], mid(tb[:, 0:ROPE], 1), ALU.mult)
                V.tensor_tensor(roq[:, :, :], gq[:, :, NOPE:QK], mid(tb[:, 0:ROPE], HEADS), ALU.mult)
                link(V.tensor_tensor(ros[:, :, :], gs[:, :, :], mid(tb[:, 2 * ROPE:2 * ROPE + SD], NS), ALU.mult))
                V.tensor_tensor(ror[:, :, :], ror[:, :, :], swr[:, :, :], ALU.add)
                V.tensor_tensor(roq[:, :, :], roq[:, :, :], swq[:, :, :], ALU.add)
                link(V.tensor_tensor(ros[:, :, :], ros[:, :, :], sws[:, :, :], ALU.add))
                V.tensor_tensor(qn[:, :, 0:NOPE], gq[:, :, 0:NOPE], bc(stn[:, 0:8], NOPE), ALU.mult)
                V.tensor_tensor(qn[:, :, NOPE:QK], roq[:, :, :], bc(stn[:, 0:8], ROPE), ALU.mult)
                V.tensor_tensor(kn[:, :, 0:NOPE], gk[:, :, :], bc(stn[:, 8:16], NOPE), ALU.mult)
                V.tensor_tensor(kn[:, :, NOPE:QK], mid(ror[:, 0, :], HEADS), bc(stn[:, 8:16], ROPE), ALU.mult)
                V.tensor_tensor(sn[:, 0:SH, :], ros[:, 0:SH, :], bc(stn[:, 16:24], SD), ALU.mult)
                for r in range(2):
                    ins = V.tensor_tensor(sn[:, SH + r::2, :], ros[:, SH:NS, :], bc(stn[:, 24:26], SD), ALU.mult)
                ins.then_inc(normed, 1)
                if not last:
                    c_norm(EV(t, 2), 1 - b)

            dve.wait_ge(consts, 16 * 6)
            link(V.tensor_scalar_add(flat(mcol[:, 1, :, :]), flat(mcol[:, 1, :, :]), 1.0))
            link(V.tensor_tensor(mcol[:, 1, :, :], mcol[:, 1, :, :], mid(gcol[:, :], 2), ALU.mult))
            x_norm(0, 0, 0)
            modulate(0, 0, 1, [0, 1])
            x_norm(1, 1, 1)
            dve.wait_ge(gains, 16 * 6)
            c_norm(2, 0)
            step(0, 0)
            step(1, 1)
            with dve.Fori(1, NT // 2 - 1) as i:
                link.enter(i - 1, 18)
                step(i * 2, 0)
                step(i * 2 + 1, 1)
                link.leave(NT // 2 - 2)
            step(NT - 2, 0)
            step(NT - 1, 1)
            lo_fills(NT)

        @block.tensor
        def _(pe):
            MM = nc.tensor.matmul

            def fill(n, bank, parts):
                if not (isinstance(n, int) and n < 2):
                    pe.wait_ge(emptied, n - 1)
                at = 0
                for x in parts:
                    m = x.shape[1]
                    last = nc.tensor.transpose(ps[0:m, TB + bank, at:at + P], x, ident[:, :])
                    at += P
                last.then_inc(filled, 1)

            def fill_x(n, banks):
                for f in range(2):
                    fill(n + f, banks[f], [xn[:, k, :] for k in range(4 * f, 4 * f + 4)])

            def fill_heads(t, k):
                if k < 7:
                    h0 = 4 * ((k - 3) % 2)
                    parts = [(qn, kn)[(k - 3) // 2][:, h, :] for h in range(h0, h0 + 4)]
                else:
                    parts = [flat(sn[:, h:h + 2, :]) for h in (4 * (k - 7), 4 * (k - 7) + 2)]
                fill(FILL(t, k), side(t, k), parts)

            def project(t, heads_of):
                pe.wait_ge(h_ready, t + 1)
                for j, (lo, hi) in enumerate(ZCH):
                    if not (isinstance(t, int) and t == 0):
                        pe.wait_ge(z_copied, t * 3 + j - 2)
                    for k in range(KC):
                        for i, (a, w) in enumerate(((0, 0), (0, 1), (1, 0))):
                            ins = MM(ps[:, j, 0:hi - lo], hT[a][:, k, :], w_in[w][:, k, lo:hi],
                                     start=(k == 0 and i == 0), stop=(k == KC - 1 and i == 2))
                        if j == 0 and k < 7 and heads_of is not None:
                            fill_heads(heads_of, k + 3)
                    ins.then_inc(z_ready, 1)

            def step(t, b):
                first = isinstance(t, int) and t == 0
                last = isinstance(t, int) and t == NT - 1
                pe.wait_ge(c_ready, t * 2 + 2)
                fill(FILL(t, 0), side(t, 0), [cn[:, i, :] for i in range(3)])
                if not last:
                    pe.wait_ge(xn_ready, t + 2)
                    fill_x(FILL(t, 1), [side(t, 1), side(t, 2)])
                pe.wait_ge(emptied, FILL(t, 0) + 1)
                for j in range(4):
                    bank = (0, 1, 2, 0)[j]
                    if j == 3:
                        pe.wait_ge(u_copied, t * 4 + 1)
                    elif not first:
                        pe.wait_ge(u_copied, t * 4 + (0, -2, -1)[j])
                    if j < 2:
                        for k in range(2):
                            for i, (a, w) in enumerate(((0, 0), (0, 1), (1, 0))):
                                ins = MM(ps[:, UB + bank, 0:4 * QK], cT[a][:, k, :], w_uq[w][:, k, j * 4 * QK:(j + 1) * 4 * QK],
                                         start=(k == 0 and i == 0), stop=(k == 1 and i == 2))
                    else:
                        for i, (a, w) in enumerate(((0, 0), (0, 1), (1, 0))):
                            ins = MM(ps[:, UB + bank, :], cT[a][:, 2, :], w_kv[w][:, (j - 2) * BANK:(j - 1) * BANK],
                                     start=(i == 0), stop=(i == 2))
                    ins.then_inc(u_ready, 1)
                if not last:
                    project(t + 1, None if first else t)
                else:
                    for k in range(3, 10):
                        fill_heads(t, k)

            pe.wait_ge(consts, 16 * 6)
            pe.wait_ge(xn_ready, 1)
            fill_x(0, [0, 1])
            project(0, None)
            for t in range(2):
                step(t, t)
            with pe.Fori(1, NT // 2 - 1) as i:
                step(i * 2, 0)
                step(i * 2 + 1, 1)
            step(NT - 2, 0)
            step(NT - 1, 1)
            pe.wait_ge(normed, NT)
            for k in range(3, 10):
                fill_heads(NT, k)


def swa_phase(nc, A, scr, mix, rs):
    with ExitStack() as ctx:
        sb = lambda n, s, d=F32: ctx.enter_context(nc.sbuf_tensor(n, s, d))
        sem = lambda n: ctx.enter_context(nc.semaphore(n))
        NKEY = UNITK * P
        UPI = 2 * SKV
        ident = sb("s_ident", [P, P])
        sink = sb("s_sink", [P, SH])
        mask = sb("s_mask", [P, 2, CTX + 3 * P + CTX])
        qs = sb("s_q", [P, UPI, GRP * P], F32R)
        kb = sb("s_k", [P, UPI, 2, NKEY], F32R)
        vb = sb("s_v", [P, UPI, UNITK, 2 * SD], F32R)
        pr = sb("s_pr", [P, 2, 2, NKEY])
        pT = [sb(f"s_pT{i}", [P, 2, UNITK, GRP, P], F32R) for i in range(2)]
        ot = sb("s_ot", [SD, 2, GRP * P])
        mx2 = sb("s_mx", [P, 2, 2])
        nb2 = sb("s_nb", [P, 2, 2])
        ds2 = sb("s_ds", [P, 2, 2])
        se2 = sb("s_se", [P, 2, 2])
        sm2 = sb("s_sm", [P, 2, 2])
        ps = ctx.enter_context(nc.psum_tensor("s_ps", [P, 8, BANK], F32))
        TB, OB = 3, 6
        consts = sem("s_consts")
        cleared = sem("s_cleared")
        loaded = [sem(f"s_loaded{i}") for i in range(UPI)]
        mask_loaded = [sem(f"s_mask_loaded{i}") for i in range(2)]
        scored = sem("s_scored")
        masked = sem("s_masked")
        shift_ready = sem("s_shift_ready")
        exped = sem("s_exped")
        filled = sem("s_filled")
        hi_ready = sem("s_hi_ready")
        emptied = sem("s_emptied")
        out_ready = sem("s_out_ready")
        out_low = sem("s_out_low")
        out_done = sem("s_out_done")
        v_chain = sem("s_v_chain")
        block = ctx.enter_context(nc.Block())
        NU = SKV * NB

        def tile_at(hh, kt):
            return P * (kt if hh == 1 else (kt + 3 if kt < 2 else kt - 2))

        FILLS = (((0, 0, 4, 0),), ((1, 0, 4, 0),), ((0, 4, 1, 0), (1, 4, 1, P)))

        @block.sync
        def _(sp):
            def load(j, u, n, wait=True):
                kv, blk, b = u // 2, j * 2 + u % 2, u
                if wait:
                    sp.wait_ge(out_ready, n - UPI + 1)
                col = blk * P
                sp.dma_start(qs[:, b, :].bitcast(F32), scr["sq"][bass.ds(blk + NCT, 1), :, kv * GRP * P:(kv + 1) * GRP * P]
                             .rearrange("a p c -> p (a c)")).then_inc(loaded[b], 16)
                sp.dma_start(kb[:, b, :, 0:CTX].bitcast(F32),
                             scr["sk"][kv, :, :, 0:CTX].rearrange("i p c -> p i c")).then_inc(loaded[b], 16)
                sp.dma_start(kb[:, b, :, CTX:NKEY].bitcast(F32),
                             scr["sk"][kv, :, :, bass.ds(col + CTX, 3 * P)].rearrange("i p c -> p i c")).then_inc(loaded[b], 16)
                sp.dma_start(vb[:, b, 0:NCT, :].bitcast(F32),
                             scr["sv"][0:NCT, :, kv * P:(kv + 1) * P].rearrange("a p c -> p a c")).then_inc(loaded[b], 16)
                sp.dma_start(vb[:, b, NCT:UNITK, :].bitcast(F32),
                             scr["sv"][bass.ds(blk + NCT, 3), :, kv * P:(kv + 1) * P].rearrange("a p c -> p a c")).then_inc(loaded[b], 16)
                if u < 2:
                    if wait:
                        sp.wait_ge(masked, n * 4 - 4)
                    sp.dma_start(mask[:, u, CTX:CTX + 3 * P],
                                 A["mask"][bass.ds(blk, 1)].rearrange("a p c -> p (a c)")).then_inc(mask_loaded[u], 16)

            sp.dma_start(ident[:, :], A["ident"]).then_inc(consts, 16)
            sp.dma_start(sink[:, :], A["swa_sink"].partition_broadcast(P).rearrange("p a n -> p (a n)")).then_inc(consts, 16)
            for u in range(UPI):
                load(0, u, u, wait=False)
            with sp.Fori(1, NB // 2) as j:
                for u in range(UPI):
                    load(j, u, j * UPI + u)

        @block.gpsimd
        def _(pool):
            for b in range(2):
                nc.gpsimd.memset(mask[:, b, 0:CTX], 0.0).then_inc(cleared, 1)
                nc.gpsimd.memset(mask[:, b, CTX + 3 * P:], 0.0).then_inc(cleared, 1)

        @block.scalar
        def _(act):
            def hi_fill(s, k, kind):
                n = s * 3 + k
                act.wait_ge(filled, n + 1)
                pair, ub = kind % 2, (kind // 2) % 2
                for hh, kt0, nk, at in FILLS[k]:
                    ins = nc.scalar.activation(pT[0][:, ub, kt0:kt0 + nk, 2 * pair + hh, :],
                                               ps[:, TB + k, at:at + nk * P].rearrange("p (k c) -> p k c", k=nk), ACT.Copy)
                ins.then_inc(hi_ready, 1)

            def out_low_copy(n, b):
                act.wait_ge(out_ready, n + 1)
                nc.scalar.activation(ot[:, b, :], ps[SD:P, OB + b, :], ACT.Copy).then_inc(out_low, 1)

            def step(s, kind, head=True, tail=True, lag=True):
                if tail:
                    if (kind - 1) % 2 == 0 and lag:
                        act.wait_ge(out_ready, (s - 1) // 2 - 1 if isinstance(s, int) else s_half(s, kind) - 1)
                    for k in range(3):
                        hi_fill(s - 1, k, kind - 1)
                if head:
                    act.wait_ge(shift_ready, s + 1)
                    nb, ds, se, sm = (x[:, kind % 2, :] for x in (nb2, ds2, se2, sm2))
                    nc.scalar.activation(se, ds, ACT.Exp)
                    for hh in range(2):
                        ins = nc.scalar.activation(pr[:, kind % 2, hh, :], pr[:, kind % 2, hh, :], ACT.Exp, bias=nb[:, hh:hh + 1],
                                                   accum_out=sm[:, hh:hh + 1])
                    ins.then_inc(exped, 1)

            def s_half(s, kind):
                return base_unit[0] + (kind - 1) // 2

            base_unit = [0]
            act.wait_ge(cleared, 4)
            SPI = 2 * UPI
            for kind in range(SPI):
                s = kind
                step(s, kind, tail=s > 0, lag=(s - 1) // 2 >= 2)
                if s >= 3 and s % 2 == 1:
                    out_low_copy((s - 3) // 2, ((s - 3) // 2) % 2)
            with act.Fori(1, NB // 2) as j:
                base_unit[0] = j * UPI
                for kind in range(SPI):
                    step(j * SPI + kind, kind)
                    if kind % 2 == 1:
                        out_low_copy(j * UPI + (kind - 3) // 2, ((kind - 3) // 2) % 2)
            S = 2 * NU
            step(S, 0, head=False)
            out_low_copy(NU - 1, 1)

        @block.vector
        def _(dve):
            V = nc.vector
            link = Chain(dve, v_chain)

            def out(n, b, kv, blk):
                dve.wait_ge(out_low, n + 1)
                for r in range(2):
                    c0 = 4 + 2 * kv
                    ins = V.tensor_tensor(mix[SD * r:SD * r + SD, c0:c0 + 2, bass.ds(blk * P, P)],
                                          ps[0:SD, OB + b, :].rearrange("p (g r c) -> p r g c", r=2, c=P)[:, r, :, :],
                                          ot[:, b, :].rearrange("p (g r c) -> p r g c", r=2, c=P)[:, r, :, :], ALU.add)
                ins.then_inc(out_done, 1)

            def lo_fill(s, k, kind):
                n = s * 3 + k
                pair, ub = kind % 2, (kind // 2) % 2
                dve.wait_ge(hi_ready, n + 1)
                for hh, kt0, nk, at in FILLS[k]:
                    ins = V.tensor_tensor(pT[1][:, ub, kt0:kt0 + nk, 2 * pair + hh, :],
                                          ps[:, TB + k, at:at + nk * P].rearrange("p (k c) -> p k c", k=nk),
                                          pT[0][:, ub, kt0:kt0 + nk, 2 * pair + hh, :].bitcast(F32), ALU.subtract)
                ins.then_inc(emptied, 1)

            def head(s, kind, blk, j):
                kv, pair, b = (kind // 4) % 2, kind % 2, (kind // 2) % 2
                h0 = kv * GRP + 2 * pair
                mx, nb, ds = (x[:, pair, :] for x in (mx2, nb2, ds2))
                if kv == 0 and pair == 0:
                    dve.wait_ge(mask_loaded[b], j * 16 + 16)
                dve.wait_ge(scored, s * 2 + 2)
                V.tensor_scalar(nb[:, :], sink[:, h0:h0 + 2], -1.0, None, ALU.mult)
                for hh in range(2):
                    m = mask[:, b, CTX:] if hh == 0 else mask[:, b, 0:NKEY]
                    src = ps[:, 0:3, :].rearrange("p a b -> p (a b)")[:, P + hh * NKEY:P + (hh + 1) * NKEY]
                    ins = V.tensor_tensor_reduce(out=pr[:, pair, hh, :], in0=src, in1=m, scale=1.0, scalar=sink[:, h0 + hh:h0 + hh + 1],
                                                 op0=ALU.add, op1=ALU.max, accum_out=mx[:, hh:hh + 1])
                ins.then_inc(masked, 2)
                dve.wait_ge(masked, s * 2 + 2)
                V.tensor_scalar(nb[:, :], mx[:, :], -1.0, None, ALU.mult)
                V.tensor_tensor(ds[:, :], sink[:, h0:h0 + 2], mx[:, :], ALU.subtract).then_inc(shift_ready, 1)

            def sums_and_low(s, kind, blk):
                kv, pair = (kind // 4) % 2, kind % 2
                h0 = kv * GRP + 2 * pair
                se, sm = (x[:, pair, :] for x in (se2, sm2))
                dve.wait_ge(exped, s + 1)
                link.mark(V.tensor_tensor(sm, sm, se, ALU.add))
                lo_fill(s, 0, kind)
                link.reach()
                link.mark(V.reciprocal(sm, sm))
                lo_fill(s, 1, kind)
                link.reach()
                link.mark(V.tensor_scalar(rs[:, bass.ds(blk, 1), HEADS + h0:HEADS + h0 + 2].rearrange("p a b -> p (a b)"),
                                          sm, 1.0, None, ALU.mult))
                lo_fill(s, 2, kind)
                link.reach()

            def body(j, s0, kinds, first):
                for kind in kinds:
                    s, blk = s0 + kind, j * 2 + (kind // 2) % 2
                    if kind == 0:
                        pkind, pblk, pj = 7, j * 2 - 1, j
                    else:
                        pkind, pblk = kind - 1, j * 2 + ((kind - 1) // 2) % 2
                    has_prev = not (first and kind == 0)
                    head(s, kind, blk, j)
                    if has_prev:
                        sums_and_low(s - 1, pkind, pblk)
                    if kind % 2 == 1 and not (first and kind < 3):
                        un = (kind - 3) // 2
                        if un >= 0:
                            out(s0 // 2 + un if isinstance(s0, int) else j * UPI + un, un % 2, un // 2, j * 2 + un % 2)
                        else:
                            out(j * UPI - 1, 1, 1, j * 2 - 1)

            dve.wait_ge(consts, 32)
            dve.wait_ge(cleared, 4)
            SPI = 2 * UPI
            body(0, 0, range(SPI), True)
            with dve.Fori(1, NB // 2) as j:
                link.enter(j - 1, 3 * SPI)
                body(j, j * SPI, range(SPI), False)
                link.leave(NB // 2 - 1)
            S, last = 2 * NU, NB // 2
            sums_and_low(S - 1, 7, NB - 1)
            out(NU - 1, 1, 1, NB - 1)

        @block.tensor
        def _(pe):
            def scores(s, kind, n, turn, wait):
                b, pair = kind // 2, kind % 2
                flat_ps = ps[:, 0:3, :].rearrange("p a b -> p (a b)")
                if pair == 0:
                    pe.wait_ge(loaded[b], turn * 80 + 80)
                if wait:
                    pe.wait_ge(masked, s * 2)
                for hh in range(2):
                    q = qs[:, b, (2 * pair + hh) * P:(2 * pair + hh + 1) * P]
                    base = P + hh * NKEY
                    ctx_at, band_at = (base + 3 * P, base) if hh == 0 else (base, base + CTX)
                    for at, lo, hi in ((band_at, CTX, NKEY), (ctx_at, 0, CTX)):
                        for i in range(2):
                            ins = nc.tensor.matmul(flat_ps[:, at:at + hi - lo], q, kb[:, b, i, lo:hi],
                                                   start=(i == 0), stop=(i == 1))
                    ins.then_inc(scored, 1)

            def transposes(s, kind, wait):
                pe.wait_ge(exped, s + 1)
                for k in range(3):
                    if wait:
                        pe.wait_ge(emptied, s * 3 + k - 2)
                    for hh, kt0, nk, at in FILLS[k]:
                        for kt in range(kt0, kt0 + nk):
                            c = tile_at(hh, kt)
                            last = nc.tensor.transpose(ps[:, TB + k, at + (kt - kt0) * P:at + (kt - kt0 + 1) * P],
                                                       pr[:, kind % 2, hh, c:c + P], ident[:, :])
                    last.then_inc(filled, 1)

            def values(n, ub, uv, s_end, wait):
                pe.wait_ge(emptied, s_end)
                if wait:
                    pe.wait_ge(out_done, n - 1)
                for kt in range(UNITK):
                    for i in range(2):
                        last = nc.tensor.matmul(ps[:, OB + ub, :], vb[:, uv, kt, :], pT[i][:, ub, kt, :, :].rearrange("p g c -> p (g c)"),
                                                start=(kt == 0 and i == 0), stop=(kt == UNITK - 1 and i == 1))
                last.then_inc(out_ready, 1)

            SPI = 2 * UPI

            def body(j, s0, turn0, first):
                for kind in range(SPI):
                    s = s0 + kind
                    turn = turn0
                    scores(s, kind, None, turn, not (first and kind == 0))
                    if not (first and kind == 0):
                        transposes(s - 1, (kind - 1) % SPI, not (first and kind == 1))
                    if kind % 2 == 1 and not (first and kind == 1):
                        un = (kind - 3) // 2
                        n = (s0 // 2 if isinstance(s0, int) else j * UPI) + un
                        values(n, un % 2, un % UPI, n * 6 + 6, not (first and un < 2))

            pe.wait_ge(consts, 32)
            body(0, 0, 0, True)
            with pe.Fori(1, NB // 2) as j:
                body(j, j * SPI, j, False)
            S = 2 * NU
            transposes(S - 1, 7, True)
            values(NU - 1, 1, UPI - 1, NU * 6, True)


def mla_phase(nc, A, scr, mix, rs):
    with ExitStack() as ctx:
        sb = lambda n, s, d=F32: ctx.enter_context(nc.sbuf_tensor(n, s, d))
        sem = lambda n: ctx.enter_context(nc.semaphore(n))
        ident = sb("l_ident", [P, P])
        qT = sb("l_q", [QK, 2, 2, SEQ], F32R)
        kT = sb("l_k", [QK, 2, 2, KALL], F32R)
        vb = sb("l_v", [P, 2, NT, 2 * VD], F32R)
        pr = sb("l_pr", [P, 2, KALL])
        pT = [sb(f"l_pT{i}", [P, 2, NT, 2, P], F32R) for i in range(2)]
        ot = sb("l_ot", [VD, 2 * P])
        nb = sb("l_nb", [P, 2])
        sm = sb("l_sm", [P, 4])
        inv = sb("l_inv", [P, 2])
        ps = ctx.enter_context(nc.psum_tensor("l_ps", [P, 8, BANK], F32))
        fps = ps[:, 0:5, :].rearrange("p a b -> p (a b)")
        TB, OB = 5, 7
        consts = sem("l_consts")
        loaded = [sem(f"l_loaded{i}") for i in range(2)]
        scored = sem("l_scored")
        shift_ready = sem("l_shift_ready")
        exped = sem("l_exped")
        shared_read = sem("l_shared_read")
        filled = sem("l_filled")
        hi_ready = sem("l_hi_ready")
        emptied = sem("l_emptied")
        out_ready = sem("l_out_ready")
        out_low = sem("l_out_low")
        out_done = sem("l_out_done")
        v_chain = sem("l_v_chain")
        block = ctx.enter_context(nc.Block())
        TILES = ((0, 4), (4, 8), (8, 10))
        SPI = 2 * NB
        TURNS = HEADS // 2
        S = HEADS * NB

        @block.sync
        def _(sp):
            def load(h, b):
                sp.dma_start(qT[:, b, :, :].bitcast(F32), scr["q"][bass.ds(h, 1), :, :, CTX:KALL]
                             .rearrange("a p i c -> p (a i) c")).then_inc(loaded[b], 16)
                sp.dma_start(kT[:, b, :, :].bitcast(F32), scr["k"][bass.ds(h, 1)]
                             .rearrange("a p i c -> p (a i) c")).then_inc(loaded[b], 16)
                sp.dma_start(vb[:, b, :, :].bitcast(F32), scr["v"][bass.ds(h, 1)]
                             .rearrange("a t p c -> p (a t) c")).then_inc(loaded[b], 16)

            sp.dma_start(ident[:, :], A["ident"]).then_inc(consts, 16)
            load(0, 0)
            load(1, 1)
            with sp.Fori(1, TURNS) as j:
                for b in range(2):
                    sp.wait_ge(out_ready, j * 8 - 4 + 4 * b)
                    load(j * 2 + b, b)

        @block.tensor
        def _(pe):
            def scores(s, kind, j, wait):
                b, qt = kind // NB, kind % NB
                if qt == 0:
                    pe.wait_ge(loaded[b], j * 48 + 48)
                if wait:
                    pe.wait_ge(exped, s - 1)
                even = kind % 2 == 0
                chunks = ((0, 0, 512), (512, 512, 1024), (1024, 1024, 1280)) if even else \
                    ((1536, 256, 768), (2048, 768, 1280), (1280, 0, 256))
                for c, (at, lo, hi) in enumerate(chunks):
                    if c == 2 and (wait or kind == 1):
                        pe.wait_ge(shared_read, s)
                    for i, (a, w) in enumerate(((0, 0), (0, 1), (1, 0))):
                        last = nc.tensor.matmul(fps[:, at:at + hi - lo], qT[:, b, a, qt * P:(qt + 1) * P],
                                                kT[:, b, w, lo:hi], start=(i == 0), stop=(i == 2))
                last.then_inc(scored, 1)

            def fill(s, kind, k, wait):
                n_par = (kind * 3 + k) % 2
                if k == 0:
                    pe.wait_ge(exped, s + 1)
                if wait:
                    pe.wait_ge(emptied, s * 3 + k - 1)
                lo, hi = TILES[k]
                for t in range(lo, hi):
                    last = nc.tensor.transpose(ps[:, TB + n_par, (t - lo) * P:(t - lo + 1) * P],
                                               pr[:, kind % 2, t * P:(t + 1) * P], ident[:, :])
                last.then_inc(filled, 1)

            def values(u, ukind, half, wait):
                b, ub = (ukind // 4) % 2, ukind % 2
                if half == 0:
                    pe.wait_ge(emptied, u * 6 + 6)
                    if wait:
                        pe.wait_ge(out_done, u)
                for t in range(NT):
                    last = nc.tensor.matmul(ps[:, OB, 0:2 * P], vb[:, b, t, :],
                                            pT[half][:, ub, t, :, :].rearrange("p q c -> p (q c)"),
                                            start=(half == 0 and t == 0), stop=(half == 1 and t == NT - 1))
                if half == 1:
                    last.then_inc(out_ready, 1)

            def turn(j, s0, u0, first):
                for kind in range(SPI):
                    s = s0 + kind
                    scores(s, kind, j, not (first and kind < 2))
                    prev = (kind - 1) % SPI
                    if not (first and kind == 0):
                        for k in range(2):
                            fill(s - 1, prev, k, not (first and kind == 1))
                    if not (first and kind < 3):
                        uk = (kind - 3) // 2
                        half = 0 if kind % 2 == 1 else 1
                        values(u0 + uk, uk % 8, half, not (first and uk == 0))
                    if not (first and kind == 0):
                        fill(s - 1, prev, 2, True)

            pe.wait_ge(consts, 16)
            turn(0, 0, 0, True)
            with pe.Fori(1, TURNS) as j:
                turn(j, j * SPI, j * 8, False)
            for k in range(2):
                fill(S - 1, SPI - 1, k, True)
            values(S // 2 - 2, 6, 1, True)
            fill(S - 1, SPI - 1, 2, True)
            values(S // 2 - 1, 7, 0, True)
            values(S // 2 - 1, 7, 1, True)

        @block.scalar
        def _(act):
            def hi_fill(s, kind, k):
                n_par = (kind * 3 + k) % 2
                ub, q2 = (kind // 2) % 2, kind % 2
                lo, hi = TILES[k]
                act.wait_ge(filled, s * 3 + k + 1)
                nc.scalar.activation(pT[0][:, ub, lo:hi, q2, :],
                                     ps[:, TB + n_par, 0:(hi - lo) * P].rearrange("p (t c) -> p t c", c=P),
                                     ACT.Copy).then_inc(hi_ready, 1)

            def turn(s0, u0, first):
                for kind in range(SPI):
                    s = s0 + kind
                    prev = (kind - 1) % SPI
                    if not (first and kind == 0):
                        if prev % 2 == 0 and not (first and kind < 5):
                            act.wait_ge(out_ready, u0 + (kind - 1) // 2 - 1)
                        for k in range(2):
                            hi_fill(s - 1, prev, k)
                    act.wait_ge(shift_ready, s + 1)
                    odd, at = kind % 2, (kind % 2) * KALL
                    parts = ((0, 256), (256, KALL)) if odd else ((1024, KALL), (0, 1024))
                    for (lo, hi), c, done in zip(parts, (odd, 2 + odd), (shared_read, exped)):
                        nc.scalar.activation(pr[:, odd, lo:hi], fps[:, at + lo:at + hi], ACT.Exp,
                                             bias=nb[:, odd:odd + 1], accum_out=sm[:, c:c + 1]).then_inc(done, 1)
                    if not (first and kind == 0):
                        hi_fill(s - 1, prev, 2)
                    if kind % 2 == 0 and not (first and kind < 4):
                        low(u0 + (kind - 4) // 2)

            def low(u):
                act.wait_ge(out_ready, u + 1)
                nc.scalar.activation(ot[:, :], ps[VD:P, OB, 0:2 * P], ACT.Copy).then_inc(out_low, 1)

            turn(0, 0, True)
            with act.Fori(1, TURNS) as j:
                turn(j * SPI, j * 8, False)
            for k in range(3):
                hi_fill(S - 1, SPI - 1, k)
            low(S // 2 - 2)
            low(S // 2 - 1)

        @block.vector
        def _(dve):
            V = nc.vector
            link = Chain(dve, v_chain)

            def lo_fill(s, kind, k):
                n_par = (kind * 3 + k) % 2
                ub, q2 = (kind // 2) % 2, kind % 2
                lo, hi = TILES[k]
                dve.wait_ge(hi_ready, s * 3 + k + 1)
                V.tensor_tensor(pT[1][:, ub, lo:hi, q2, :],
                                ps[:, TB + n_par, 0:(hi - lo) * P].rearrange("p (t c) -> p t c", c=P),
                                pT[0][:, ub, lo:hi, q2, :].bitcast(F32), ALU.subtract).then_inc(emptied, 1)

            def out(u, h, uk):
                r, q0 = (uk // 4) % 2, (uk % 4) * 2 * P
                dve.wait_ge(out_low, u + 1)
                V.tensor_tensor(mix[VD * r:VD * r + VD, bass.ds(h, 1), q0:q0 + 2 * P].rearrange("p a c -> p (a c)"),
                                ps[0:VD, OB, 0:2 * P], ot[:, :], ALU.add).then_inc(out_done, 1)

            def total_and_low(s, kind, j):
                dve.wait_ge(exped, s + 1)
                c = kind % 2
                link.mark(V.tensor_tensor(inv[:, c:c + 1], sm[:, c:c + 1], sm[:, 2 + c:3 + c], ALU.add))
                lo_fill(s, kind, 0)
                link.reach()
                link.mark(V.reciprocal(inv[:, c:c + 1], inv[:, c:c + 1]))
                lo_fill(s, kind, 1)
                link.reach()
                V.tensor_scalar(rs[:, kind % NB, bass.ds(j * 2 + kind // NB, 1)], inv[:, c:c + 1], 1.0, None, ALU.mult)
                lo_fill(s, kind, 2)

            def turn(j, s0, u0, first):
                for kind in range(SPI):
                    s = s0 + kind
                    prev = (kind - 1) % SPI
                    pj = j - 1 if kind == 0 else j
                    dve.wait_ge(scored, s + 1)
                    V.tensor_reduce(nb[:, kind % 2:kind % 2 + 1], fps[:, (kind % 2) * KALL:(kind % 2 + 1) * KALL],
                                    AX.X, ALU.max, negate=True).then_inc(shift_ready, 1)
                    if not (first and kind == 0):
                        total_and_low(s - 1, prev, pj)
                    if kind % 2 == 0 and not (first and kind < 4):
                        uk = (kind - 4) // 2
                        out(u0 + uk, j - 1 if uk < 0 else j, uk % 8)

            turn(0, 0, 0, True)
            with dve.Fori(1, TURNS) as j:
                link.enter(j - 1, 2 * SPI)
                turn(j, j * SPI, j * 8, False)
                link.leave(TURNS - 1)
            total_and_low(S - 1, SPI - 1, TURNS - 1)
            out(S // 2 - 2, TURNS - 1, 6)
            out(S // 2 - 1, TURNS - 1, 7)


def out_phase(nc, A, scr, mix, rs, h2):
    with ExitStack() as ctx:
        sb = lambda n, s, d=F32: ctx.enter_context(nc.sbuf_tensor(n, s, d))
        sem = lambda n: ctx.enter_context(nc.semaphore(n))
        WR = 4
        w_out = [sb(f"o_w{i}", [P, KC, D], F32R) for i in range(2)]
        raw = sb("o_raw", [P, WR, D])
        ident = sb("o_ident", [P, P])
        g1 = sb("o_g1", [P, D])
        mcol = sb("o_mcol", [P, 2, KC])
        gcol = sb("o_gcol", [P, KC])
        rb = sb("o_rb", [P, HEADS + SH, VD])
        mn = sb("o_mn", [P, KC, P])
        mT = h2
        xt = sb("o_x", [P, D])
        x1 = sb("o_x1", [P, D])
        xn = sb("o_xn", [P, KC, P])
        st = sb("o_st", [P, 1])
        ps = ctx.enter_context(nc.psum_tensor("o_ps", [P, 8, BANK], F32))
        BB, TB = 0, 4
        YB = (2, 6)
        consts = sem("o_consts")
        w_loaded = [sem(f"o_w_loaded{i}") for i in range(WR)]
        w_hi = sem("o_w_hi")
        w_lo = sem("o_w_lo")
        x_loaded = sem("o_x_loaded")
        widened = sem("o_widened")
        spread = sem("o_spread")
        scaled = sem("o_scaled")
        m_hi = sem("o_m_hi")
        m_ready = sem("o_m_ready")
        y_ready = sem("o_y_ready")
        gated = sem("o_gated")
        x1_ready = sem("o_x1_ready")
        squared = sem("o_squared")
        var_ready = sem("o_var_ready")
        root_ready = sem("o_root_ready")
        xn_ready = sem("o_xn_ready")
        turned = sem("o_turned")
        scaled_h = sem("o_scaled_h")
        hv_ready = sem("o_hv_ready")
        h_hi = sem("o_h_hi")
        h_ready = sem("o_h_ready")
        stored = sem("o_stored")
        v_chain = sem("o_v_chain")
        block = ctx.enter_context(nc.Block())

        @block.sync
        def _(sp):
            def consts_in():
                sp.dma_start(g1[:, :], scr["mod"][0:1, 2 * D:3 * D].partition_broadcast(P).rearrange("p a n -> p (a n)")).then_inc(consts, 16)
                with nc.allow_non_contiguous_dma(reason="a few vectors, one element a row"):
                    sp.dma_start(gcol[:, :], A["g_mlp"].rearrange("l (k p) -> p (l k)", p=P)).then_inc(consts, 16)
                    for s in range(2):
                        sp.dma_start(mcol[:, s, :],
                                     scr["mod"][0, (3 + s) * D:(4 + s) * D].rearrange("(k p) -> p k", p=P)).then_inc(consts, 16)

            sp.dma_start(ident[:, :], A["ident"]).then_inc(consts, 16)
            for k in range(KC):
                if k == WR:
                    consts_in()
                if k >= WR:
                    sp.wait_ge(w_lo, k - WR + 1)
                sp.dma_start(raw[:, k % WR, :], A["w_out"][0, k * P:(k + 1) * P, :]).then_inc(w_loaded[k % WR], 16)
            for t in range(NB):
                if t:
                    sp.wait_ge(x1_ready, t)
                sp.dma_start(xt[:, :], A["x"][0, t * P:(t + 1) * P, :]).then_inc(x_loaded, 16)
                if t:
                    sp.dma_start(scr["x1"][(t - 1) * P:t * P, :], x1[:, :]).then_inc(stored, 16)
            sp.wait_ge(x1_ready, NB)
            sp.dma_start(scr["x1"][(NB - 1) * P:, :], x1[:, :]).then_inc(stored, 16)
            sp.wait_ge(stored, 16 * NB)

        @block.gpsimd
        def _(pool):
            for t in range(NB):
                if t:
                    pool.wait_ge(spread, 2 * t)
                nc.gpsimd.tensor_copy(rb[:, :, :], bc(rs[:, t, :], VD)).then_inc(widened, 1)

        @block.scalar
        def _(act):
            def high_w(ks):
                for k in ks:
                    act.wait_ge(w_loaded[k % WR], 16 * (k // WR + 1))
                    nc.scalar.activation(w_out[0][:, k, :], raw[:, k % WR, :], ACT.Copy).then_inc(w_hi, 1)

            def high_mix(t):
                act.wait_ge(scaled, 2 * t + 2)
                nc.scalar.activation(mT[0][:, :, t * P:(t + 1) * P], mn[:, :, :], ACT.Copy).then_inc(m_hi, 1)

            high_w(range(4))
            high_mix(0)
            high_w(range(4, KC))
            high_mix(1)
            act.wait_ge(w_lo, KC)
            for t in range(NB):
                act.wait_ge(x1_ready, t + 1)
                nc.scalar.activation(raw[:, 0, :], x1[:, :], ACT.Square, accum_out=st[:, :]).then_inc(squared, 1)
                act.wait_ge(var_ready, t + 1)
                nc.scalar.activation(st[:, :], st[:, :], ACT.Sqrt).then_inc(root_ready, 1)
                if t + 2 < NB:
                    high_mix(t + 2)
                act.wait_ge(hv_ready, t + 1)
                nc.scalar.activation(h2[0][:, :, t * P:(t + 1) * P], xn[:, :, :], ACT.Copy).then_inc(h_hi, 1)

        @block.vector
        def _(dve):
            V = nc.vector
            link = Chain(dve, v_chain)
            def low_w(ks):
                for k in ks:
                    dve.wait_ge(w_hi, k + 1)
                    V.tensor_tensor(w_out[1][:, k, :], raw[:, k % WR, :], w_out[0][:, k, :].bitcast(F32),
                                    ALU.subtract).then_inc(w_lo, 1)

            def scale_mix(t):
                if t:
                    dve.wait_ge(m_ready, t)
                for f in range(2):
                    dve.wait_ge(spread, 2 * t + f + 1)
                    V.tensor_tensor(mn[:, 4 * f:4 * f + 4, :], ps[:, BB + f, :].rearrange("p (k c) -> p k c", k=4),
                                    mix[:, 4 * f:4 * f + 4, t * P:(t + 1) * P], ALU.mult).then_inc(scaled, 1)

            def low_mix(t):
                dve.wait_ge(m_hi, t + 1)
                V.tensor_tensor(mT[1][:, :, t * P:(t + 1) * P], mn[:, :, :], mT[0][:, :, t * P:(t + 1) * P].bitcast(F32),
                                ALU.subtract).then_inc(m_ready, 1)

            low_w(range(4))
            scale_mix(0)
            low_mix(0)
            low_w(range(4, KC))
            scale_mix(1)
            low_mix(1)
            dve.wait_ge(consts, 16 * 5)
            link(V.tensor_scalar_add(mcol[:, 1, :], mcol[:, 1, :], 1.0))
            link(V.tensor_tensor(mcol[:, 1, :], mcol[:, 1, :], gcol[:, :], ALU.mult))
            for t in range(NB):
                dve.wait_ge(y_ready, 2 * t + 2)
                if t:
                    dve.wait_ge(stored, 16 * t)
                V.tensor_tensor(x1[:, :], flat(ps[:, YB[t % 2]:YB[t % 2] + 2, :]), g1[:, :], ALU.mult).then_inc(gated, 1)
                dve.wait_ge(gated, t + 1)
                dve.wait_ge(x_loaded, 16 * t + 16)
                V.tensor_tensor(x1[:, :], x1[:, :], xt[:, :], ALU.add).then_inc(x1_ready, 1)
                dve.wait_ge(squared, t + 1)
                V.tensor_scalar(st[:, :], st[:, :], 1.0 / D, EPS, ALU.mult, ALU.add).then_inc(var_ready, 1)
                dve.wait_ge(root_ready, t + 1)
                link(V.reciprocal(st[:, :], st[:, :]))
                V.tensor_scalar(flat(xn[:, :, :]), x1[:, :], st[:, 0:1], None, ALU.mult).then_inc(xn_ready, 1)
                if t + 2 < NB:
                    scale_mix(t + 2)
                    low_mix(t + 2)
                for f in range(2):
                    dve.wait_ge(turned, 2 * t + f + 1)
                    V.tensor_tensor(xn[:, 4 * f:4 * f + 4, :], ps[:, TB + f, :].rearrange("p (k c) -> p k c", k=4),
                                    bc(mcol[:, 1, 4 * f:4 * f + 4], P), ALU.mult).then_inc(scaled_h, 1)
                dve.wait_ge(scaled_h, 2 * t + 2)
                V.tensor_tensor(xn[:, :, :], xn[:, :, :], bc(mcol[:, 0, :], P), ALU.add).then_inc(hv_ready, 1)
                dve.wait_ge(h_hi, t + 1)
                V.tensor_tensor(h2[1][:, :, t * P:(t + 1) * P], xn[:, :, :], h2[0][:, :, t * P:(t + 1) * P].bitcast(F32),
                                ALU.subtract).then_inc(h_ready, 1)

        @block.tensor
        def _(pe):
            def spread_sums(t):
                pe.wait_ge(widened, t + 1)
                for f in range(2):
                    if t:
                        pe.wait_ge(scaled, 2 * t - 1 + f)
                    for c in range(4):
                        k = 4 * f + c
                        last = nc.tensor.transpose(ps[:, BB + f, c * P:(c + 1) * P], flat(rb[:, 2 * k:2 * k + 2, :]), ident[:, :])
                    last.then_inc(spread, 1)

            def project(t):
                pe.wait_ge(m_ready, t + 1)
                if t >= 2:
                    pe.wait_ge(gated, t - 1)
                for half in range(2):
                    for k in range(KC):
                        if t == 0 and half == 0:
                            pe.wait_ge(w_lo, k + 1)
                        for i, (a, w) in enumerate(((0, 0), (0, 1), (1, 0))):
                            last = nc.tensor.matmul(ps[:, YB[t % 2] + half, :], mT[a][:, k, t * P:(t + 1) * P],
                                                    w_out[w][:, k, half * BANK:(half + 1) * BANK],
                                                    start=(k == 0 and i == 0), stop=(k == KC - 1 and i == 2))
                    last.then_inc(y_ready, 1)

            pe.wait_ge(consts, 16 * 5)
            spread_sums(0)
            spread_sums(1)
            project(0)
            for t in range(NB):
                if t + 2 < NB:
                    spread_sums(t + 2)
                if t + 1 < NB:
                    project(t + 1)
                pe.wait_ge(xn_ready, t + 1)
                if t:
                    pe.wait_ge(hv_ready, t)
                for f in range(2):
                    for c in range(4):
                        last = nc.tensor.transpose(ps[:, TB + f, c * P:(c + 1) * P], xn[:, 4 * f + c, :], ident[:, :])
                    last.then_inc(turned, 1)


def mlp_phase(nc, A, scr, h2, out):
    with ExitStack() as ctx:
        sb = lambda n, s, d=F32: ctx.enter_context(nc.sbuf_tensor(n, s, d))
        sem = lambda n: ctx.enter_context(nc.semaphore(n))
        FC = 4
        NCH = NF // FC
        acc = sb("f_acc", [P, NB, D])
        g2 = sb("f_g2", [P, D])
        w1r = sb("f_w1r", [P, KC, P])
        w2r = sb("f_w2r", [P, D])
        w1 = [sb(f"f_w1{i}", [P, 2, KC, P], F32R) for i in range(2)]
        w2 = [sb(f"f_w2{i}", [P, FC, D], F32R) for i in range(2)]
        r = sb("f_r", [P, SEQ])
        a = sb("f_a", [P, SEQ])
        aT = [sb(f"f_aT{i}", [P, FC, SEQ], F32R) for i in range(2)]
        tmp = sb("f_tmp", [P, D])
        ps = ctx.enter_context(nc.psum_tensor("f_ps", [P, 8, BANK], F32))
        consts = sem("f_consts")
        acc_loaded = sem("f_acc_loaded")
        w1_loaded = sem("f_w1_loaded")
        w2_loaded = sem("f_w2_loaded")
        w1_hi = sem("f_w1_hi")
        w1_ready = sem("f_w1_ready")
        w2_hi = sem("f_w2_hi")
        w2_ready = sem("f_w2_ready")
        up_ready = sem("f_up_ready")
        rect = sem("f_rect")
        a_hi = sem("f_a_hi")
        a_square = sem("f_a_square")
        a_ready = sem("f_a_ready")
        down_ready = sem("f_down_ready")
        gated = sem("f_gated")
        added = sem("f_added")
        stored = sem("f_stored")
        block = ctx.enter_context(nc.Block())
        w1_dram = A["w_mlp1"][0].rearrange("(k p) (f c) -> f p k c", p=P, c=P)
        w2_dram = A["w_mlp2"][0].rearrange("(f p) n -> f p n", p=P)

        @block.sync
        def _(sp):
            def load_w1(g, wait=True):
                if wait:
                    sp.wait_ge(w1_ready, g)
                sp.dma_start(w1r[:, :, :], w1_dram[bass.ds(g, 1)].rearrange("f p k c -> p (f k) c")).then_inc(w1_loaded, 16)

            def load_w2(g, wait=True):
                if wait:
                    sp.wait_ge(w2_ready, g)
                sp.dma_start(w2r[:, :], w2_dram[bass.ds(g, 1)].rearrange("f p n -> p (f n)")).then_inc(w2_loaded, 16)

            load_w1(0, wait=False)
            load_w2(0, wait=False)
            sp.dma_start(g2[:, :], scr["mod"][0:1, 5 * D:6 * D].partition_broadcast(P).rearrange("p a n -> p (a n)")).then_inc(consts, 16)
            sp.dma_start(acc[:, :, :], scr["x1"].rearrange("(t p) n -> p t n", p=P)).then_inc(acc_loaded, 16)
            load_w1(1)
            load_w2(1)
            with sp.Fori(2, NF) as g:
                load_w1(g)
                load_w2(g)
            for t in range(NB):
                sp.wait_ge(added, (NCH - 1) * NB + t + 1)
                sp.dma_start(out[0, t * P:(t + 1) * P, :], acc[:, t, :]).then_inc(stored, 16)
            sp.wait_ge(stored, 16 * NB)

        @block.scalar
        def _(act):
            def w1_high(g, slot, wait=True):
                act.wait_ge(w1_loaded, g * 16 + 16)
                if wait:
                    act.wait_ge(up_ready, g - 1)
                nc.scalar.activation(w1[0][:, slot, :, :], w1r[:, :, :], ACT.Copy).then_inc(w1_hi, 1)

            def w2_high(g, f, ch, wait=True):
                act.wait_ge(w2_loaded, g * 16 + 16)
                if wait and f == 0:
                    act.wait_ge(down_ready, ch * NB)
                nc.scalar.activation(w2[0][:, f, :], w2r[:, :], ACT.Copy).then_inc(w2_hi, 1)

            def turn(ch, g0, first, last):
                for f in range(FC):
                    g = g0 + f
                    if not (last and f == FC - 1):
                        w1_high(g + 1, (f + 1) % 2, wait=not (first and f == 0))
                    w2_high(g, f, ch, wait=not first)
                    act.wait_ge(up_ready, g + 1)
                    if not (first and f == 0):
                        act.wait_ge(a_ready, g)
                    b = 2 * (f % 2)
                    nc.scalar.activation(r[:, :], flat(ps[:, b:b + 2, :]), ACT.Relu).then_inc(rect, 1)
                    act.wait_ge(rect, g + 1)
                    nc.scalar.activation(aT[0][:, f, :], r[:, :], ACT.Square).then_inc(a_hi, 1)

            w1_high(0, 0, wait=False)
            turn(0, 0, True, False)
            with act.Fori(1, NCH - 1) as ch:
                turn(ch, ch * FC, False, False)
            turn(NCH - 1, NF - FC, False, True)

        @block.vector
        def _(dve):
            V = nc.vector

            def w1_low(g, slot):
                dve.wait_ge(w1_hi, g + 1)
                V.tensor_tensor(w1[1][:, slot, :, :], w1r[:, :, :], w1[0][:, slot, :, :].bitcast(F32),
                                ALU.subtract).then_inc(w1_ready, 1)

            def turn(ch, g0, first, last):
                for f in range(FC):
                    g = g0 + f
                    if not (last and f == FC - 1):
                        w1_low(g + 1, (f + 1) % 2)
                    dve.wait_ge(w2_hi, g + 1)
                    V.tensor_tensor(w2[1][:, f, :], w2r[:, :], w2[0][:, f, :].bitcast(F32), ALU.subtract).then_inc(w2_ready, 1)
                    dve.wait_ge(rect, g + 1)
                    if not (first and f == 0):
                        dve.wait_ge(a_ready, g)
                    V.tensor_tensor(a[:, :], r[:, :], r[:, :], ALU.mult).then_inc(a_square, 1)
                    dve.wait_ge(a_square, g + 1)
                    dve.wait_ge(a_hi, g + 1)
                    V.tensor_tensor(aT[1][:, f, :], a[:, :], aT[0][:, f, :].bitcast(F32), ALU.subtract).then_inc(a_ready, 1)
                for t in range(NB):
                    n = ch * NB + t
                    dve.wait_ge(down_ready, n + 1)
                    b = 4 + 2 * (t % 2)
                    if not (first and t == 0):
                        dve.wait_ge(added, n)
                    V.tensor_tensor(tmp[:, :], flat(ps[:, b:b + 2, :]), g2[:, :], ALU.mult).then_inc(gated, 1)
                    dve.wait_ge(gated, n + 1)
                    V.tensor_tensor(acc[:, t, :], acc[:, t, :], tmp[:, :], ALU.add).then_inc(added, 1)

            w1_low(0, 0)
            dve.wait_ge(consts, 16)
            dve.wait_ge(acc_loaded, 16)
            turn(0, 0, True, False)
            with dve.Fori(1, NCH - 1) as ch:
                turn(ch, ch * FC, False, False)
            turn(NCH - 1, NF - FC, False, True)

        @block.tensor
        def _(pe):
            def up(g, f, wait):
                slot, b = f % 2, 2 * (f % 2)
                pe.wait_ge(w1_ready, g + 1)
                if wait:
                    pe.wait_ge(rect, g - 1)
                for k in range(KC):
                    for i, (x, w) in enumerate(((0, 0), (1, 0), (0, 1))):
                        for half in range(2):
                            last = nc.tensor.matmul(ps[:, b + half, :], w1[w][:, slot, k, :],
                                                    h2[x][:, k, half * BANK:(half + 1) * BANK],
                                                    start=(k == 0 and i == 0), stop=(k == KC - 1 and i == 2))
                last.then_inc(up_ready, 1)

            def down(n, t, g0, wait):
                b = 4 + 2 * (t % 2)
                if wait:
                    pe.wait_ge(gated, n - 1)
                for f in range(FC):
                    if t == 0:
                        pe.wait_ge(a_ready, g0 + f + 1)
                        pe.wait_ge(w2_ready, g0 + f + 1)
                    for i, (x, w) in enumerate(((0, 0), (0, 1), (1, 0))):
                        for half in range(2):
                            last = nc.tensor.matmul(ps[:, b + half, :], aT[x][:, f, t * P:(t + 1) * P],
                                                    w2[w][:, f, half * BANK:(half + 1) * BANK],
                                                    start=(f == 0 and i == 0), stop=(f == FC - 1 and i == 2))
                last.then_inc(down_ready, 1)

            def turn(ch, g0, first):
                for f in range(FC):
                    up(g0 + f, f, not (first and f < 2))
                for t in range(NB):
                    down(ch * NB + t, t, g0, not (first and t < 2))

            turn(0, 0, True)
            with pe.Fori(1, NCH) as ch:
                turn(ch, ch * FC, False)


def layer(nc, A, out):
    scratch = lambda n, s: nc.dram_tensor(f"scratch_{n}", s, F32, kind="Internal").ap()
    scr = {
        "mod": scratch("mod", (2, 6 * D)),
        "q": scratch("q", (HEADS, QK, 2, KALL)),
        "k": scratch("k", (HEADS, QK, 2, KALL)),
        "v": scratch("v", (HEADS, NT, P, 2 * VD)),
        "sq": scratch("sq", (NT, P, SH * P)),
        "sk": scratch("sk", (SKV, 2, P, CTX + SEQ + 2 * P)),
        "sv": scratch("sv", (NT + 2, P, SKV * P)),
        "x1": scratch("x1", (SEQ, D)),
    }
    token_phase(nc, A, scr)
    with ExitStack() as ctx:
        h2 = [ctx.enter_context(nc.sbuf_tensor(f"h2_{i}", [P, KC, SEQ], F32R)) for i in range(2)]
        with ExitStack() as inner:
            mix = inner.enter_context(nc.sbuf_tensor("mix", [P, KC, SEQ], F32))
            rs = inner.enter_context(nc.sbuf_tensor("rs", [P, NB, HEADS + SH], F32))
            swa_phase(nc, A, scr, mix, rs)
            mla_phase(nc, A, scr, mix, rs)
            out_phase(nc, A, scr, mix, rs, h2)
        mlp_phase(nc, A, scr, h2, out)


INS = ["x", "c", "ctx", "c_ctx", "w_mod", "b_mod", "g_attn", "w_in", "g_q_a", "w_uq", "g_kv_a", "w_ukv", "g_mla_q",
       "g_mla_k", "g_swa_q", "g_swa_k", "swa_sink", "w_out", "g_mlp", "w_mlp1", "w_mlp2"]


def shape_constants():
    import numpy as np
    grid = 64

    def rope(dim):
        n = dim // 4
        inv = (np.float32(10000.0) ** (-np.arange(n, dtype=np.float32) / np.float32(n))).astype(np.float32)
        tok = np.arange(SEQ)
        row, col = (tok // grid).astype(np.float32), (tok % grid).astype(np.float32)
        ang = np.concatenate([row[:, None] * inv, col[:, None] * inv], axis=1).astype(np.float32).astype(np.float64)
        cos, sin = np.cos(ang), np.sin(ang)
        cos = np.concatenate([np.ones((CTX, dim // 2)), cos]).astype(np.float32)
        sin = np.concatenate([np.zeros((CTX, dim // 2)), sin]).astype(np.float32)
        return np.concatenate([cos, cos, -sin, sin], axis=1)

    table = np.concatenate([rope(ROPE), rope(SD)], axis=1).astype(np.float32)
    q = np.arange(P)[None, :, None] + P * np.arange(NB)[:, None, None]
    k = np.arange(3 * P)[None, None, :] - P + P * np.arange(NB)[:, None, None]
    valid = (np.abs(q - k) <= P) & (k >= 0) & (k < SEQ)
    return {"ident": np.eye(P, dtype=np.float32), "rope": table,
            "mask": np.where(valid, np.float32(0), np.float32(-1e30)).astype(np.float32)}


def kernel(**inputs):
    import numpy as np
    import concourse.bacc as bacc
    from concourse.bass_utils import run_bass_kernel_spmd

    nc = bacc.Bacc("TRN2", target_bir_lowering=False, num_devices=1)
    host = {n: np.ascontiguousarray(inputs[n]) for n in INS}
    host.update(shape_constants())
    arrays = {f"in_{n}": v for n, v in host.items()}
    A = {n: nc.dram_tensor(f"in_{n}", v.shape, mybir.dt.from_np(v.dtype), kind="ExternalInput").ap() for n, v in host.items()}
    out = nc.dram_tensor("out_0", (1, SEQ, D), F32, kind="ExternalOutput").ap()
    layer(nc, A, out)
    r = run_bass_kernel_spmd(nc, [arrays], core_ids=[0])
    return r.results[0]["out_0"]
```
